# Optimizing a Trainium2 kernel written in Bass

```python
import jax, jax.numpy as jnp
from jax import lax
import numpy as np

D_MODEL = 1024
BATCH = 1
SEQ = 1024
DEPTH = 1
DEC_BATCH = 1
DEC_SEQ = 64
PAST_LEN = 512

CHUNK = 64
D_A = 512
D_B = 512
CONV_A = 31
CONV_B = 3
D_FF = 2816
CONV_F = 3
D_IN = 2 * D_A + 3 * D_B + 2 * D_MODEL
RMS_EPS = 1e-6
LN_EPS = 1e-5

kernel_name = "gated_parallel_conv_streaming_encoder"

def rms_norm(x, g):
    x32 = x.astype(jnp.float32)
    y = x32 * lax.rsqrt(jnp.mean(x32 * x32, axis=-1, keepdims=True) + RMS_EPS)
    return (y * g.astype(jnp.float32)).astype(x.dtype)

def layer_norm(x, g, b):
    x32 = x.astype(jnp.float32)
    mu = jnp.mean(x32, axis=-1, keepdims=True)
    xc = x32 - mu
    var = jnp.mean(xc * xc, axis=-1, keepdims=True)
    y = xc * lax.rsqrt(var + LN_EPS) * g.astype(jnp.float32) + b.astype(jnp.float32)
    return y.astype(x.dtype)

def causal_dwconv(h, prev, w):
    width, ch = w.shape
    hp = jnp.concatenate([prev.astype(h.dtype), h], axis=1)
    y = lax.conv_general_dilated(
        hp, w[:, None, :].astype(h.dtype), window_strides=(1,), padding="VALID",
        dimension_numbers=("NWC", "WIO", "NWC"), feature_group_count=ch)
    return y, hp[:, hp.shape[1] - (width - 1):, :]

def layer(x, st_a, st_b, st_f, norm1_g, w_in, b_gate, dw_a, b_dw_a, ln_a_g, ln_a_b, w_a_out,
          dw_b, w_b_out, w_o, norm2_g, w_up, dw_f, w_down):
    h = rms_norm(x, norm1_g)
    z = h @ w_in
    a_val, a_gate, b_g, c_g, b_val, gates = jnp.split(
        z, [D_A, 2 * D_A, 2 * D_A + D_B, 2 * D_A + 2 * D_B, 2 * D_A + 3 * D_B], axis=-1)
    u = a_val * jax.nn.sigmoid(a_gate)
    u, new_a = causal_dwconv(u, st_a, dw_a)
    u = jax.nn.silu(layer_norm(u + b_dw_a, ln_a_g, ln_a_b))
    y_a = u @ w_a_out
    v, new_b = causal_dwconv(c_g * b_val, st_b, dw_b)
    y_b = (b_g * v) @ w_b_out
    g = jax.nn.sigmoid(gates + b_gate)
    g_a, g_b = jnp.split(g, 2, axis=-1)
    x = x + (g_a * y_a + g_b * y_b) @ w_o
    h = rms_norm(x, norm2_g)
    f_gate, f_val = jnp.split(h @ w_up, 2, axis=-1)
    f_gate, new_f = causal_dwconv(f_gate, st_f, dw_f)
    x = x + (jax.nn.silu(f_gate) * f_val) @ w_down
    return x, new_a, new_b, new_f

def setup_inputs(seed: int = 0) -> dict:
    key = jax.random.key(seed)
    ks = jax.random.split(key, 24)
    f32 = jnp.float32
    nrm = lambda k, shape, s: jax.random.normal(k, shape, f32) * s
    return {
        "x_prompt": nrm(ks[0], (BATCH, SEQ, D_MODEL), 1.0),
        "x_sample": nrm(ks[1], (DEC_BATCH, DEC_SEQ, D_MODEL), 1.0),
        "cache_conv_a": nrm(ks[2], (DEPTH, DEC_BATCH, CONV_A - 1, D_A), 0.5),
        "cache_conv_b": nrm(ks[3], (DEPTH, DEC_BATCH, CONV_B - 1, D_B), 0.5),
        "cache_ffn_conv": nrm(ks[4], (DEPTH, DEC_BATCH, CONV_F - 1, D_FF), 0.5),
        "norm1_g": 1.0 + nrm(ks[5], (DEPTH, D_MODEL), 0.02),
        "w_in": nrm(ks[6], (DEPTH, D_MODEL, D_IN), D_MODEL ** -0.5),
        "b_gate": nrm(ks[7], (DEPTH, 2 * D_MODEL), 0.02),
        "dw_a": nrm(ks[8], (DEPTH, CONV_A, D_A), CONV_A ** -0.5),
        "b_dw_a": nrm(ks[9], (DEPTH, D_A), 0.02),
        "ln_a_g": 1.0 + nrm(ks[10], (DEPTH, D_A), 0.02),
        "ln_a_b": nrm(ks[11], (DEPTH, D_A), 0.02),
        "w_a_out": nrm(ks[12], (DEPTH, D_A, D_MODEL), D_A ** -0.5),
        "dw_b": nrm(ks[13], (DEPTH, CONV_B, D_B), CONV_B ** -0.5),
        "w_b_out": nrm(ks[14], (DEPTH, D_B, D_MODEL), D_B ** -0.5),
        "w_o": nrm(ks[15], (DEPTH, D_MODEL, D_MODEL), D_MODEL ** -0.5),
        "norm2_g": 1.0 + nrm(ks[16], (DEPTH, D_MODEL), 0.02),
        "w_up": nrm(ks[17], (DEPTH, D_MODEL, 2 * D_FF), D_MODEL ** -0.5),
        "dw_f": nrm(ks[18], (DEPTH, CONV_F, D_FF), CONV_F ** -0.5),
        "w_down": nrm(ks[19], (DEPTH, D_FF, D_MODEL), D_FF ** -0.5),
        "final_g": 1.0 + nrm(ks[20], (D_MODEL,), 0.02),
    }

def reference(x_prompt, x_sample, cache_conv_a, cache_conv_b, cache_ffn_conv, norm1_g, w_in, b_gate,
              dw_a, b_dw_a, ln_a_g, ln_a_b, w_a_out, dw_b, w_b_out, w_o, norm2_g, w_up, dw_f,
              w_down, final_g):
    n_p = x_prompt.shape[0]
    dt = x_prompt.dtype
    zero_a = jnp.zeros((n_p, CONV_A - 1, D_A), dt)
    zero_b = jnp.zeros((n_p, CONV_B - 1, D_B), dt)
    zero_f = jnp.zeros((n_p, CONV_F - 1, D_FF), dt)
    xp, xs = x_prompt, x_sample
    pa, pb, pf, sa, sb, sf = [], [], [], [], [], []
    for l in range(DEPTH):
        w_l = (norm1_g[l], w_in[l], b_gate[l], dw_a[l], b_dw_a[l], ln_a_g[l], ln_a_b[l], w_a_out[l],
               dw_b[l], w_b_out[l], w_o[l], norm2_g[l], w_up[l], dw_f[l], w_down[l])
        xp, na, nb, nf = layer(xp, zero_a, zero_b, zero_f, *w_l)
        pa.append(na); pb.append(nb); pf.append(nf)
        xs, na, nb, nf = layer(xs, cache_conv_a[l], cache_conv_b[l], cache_ffn_conv[l], *w_l)
        sa.append(na); sb.append(nb); sf.append(nf)
    y_prompt = rms_norm(xp, final_g)
    y_sample = rms_norm(xs, final_g)
    return (y_prompt, y_sample, jnp.stack(pa), jnp.stack(pb), jnp.stack(pf),
            jnp.stack(sa), jnp.stack(sb), jnp.stack(sf))


_drawn_inputs = setup_inputs


def setup_inputs(seed=0):
    import zlib

    import numpy as np

    out = dict(_drawn_inputs(seed))
    spreads = {}
    factors = {'b_gate': 8.0,
     'b_dw_a': 4.783,
     'ln_a_g': 7.39,
     'ln_a_b': 8.0,
     'norm2_g': 2.858,
     'final_g': 8.677,
     'cache_conv_b': 3.299}
    for name, (base, spread) in spreads.items():
        noise = np.random.default_rng([zlib.crc32(name.encode()), seed]).standard_normal(out[name].shape)
        drawn = base * np.exp(spread * noise) if base else spread * noise
        out[name] = __import__('jax').numpy.asarray(drawn.astype(out[name].dtype))
    for name, factor in factors.items():
        out[name] = (out[name] * factor).astype(out[name].dtype)
    return out
```

```python
from contextlib import ExitStack

import concourse.bass as bass
from concourse import mybir

F32 = mybir.dt.float32
F32R = mybir.dt.float32r
ALU = mybir.AluOpType
ACT = mybir.ActivationFunctionType

P = 128
CHUNKS = 3


def streaming_encoder(nc: bass.Bass, ins, outs):
    D = ins["x_prompt"].shape[2]
    NP = ins["x_prompt"].shape[1]
    NS = ins["x_sample"].shape[1]
    TAPS_A, DA = ins["dw_a"].shape[1:]
    TAPS_B, DB = ins["dw_b"].shape[1:]
    TAPS_F, DF = ins["dw_f"].shape[1:]
    RMS_EPS, LN_EPS = 1e-6, 1e-5
    KD, KA, KB, KF = D // P, DA // P, DB // P, DF // P
    HA, H = TAPS_A - 1, TAPS_B - 1
    assert TAPS_F == TAPS_B == 3 and KA == KB == 4 and KD == 8 and KF % 2 == 0

    P0 = H
    S0 = 2 * H + NP
    W = S0 + NS
    CW = W // CHUNKS
    assert CW * CHUNKS == W and CW % 2 == 0 and CW <= 512
    UW = 2 * HA + NP + NS
    CVW = UW - HA
    US = 2 * HA + NP
    CS = HA + NP
    TILES = [(0, r, P, P0 + r) for r in range(0, NP, P)] + [(1, 0, NS, S0)]
    NT = len(TILES)
    SW = NT * P

    N_A = 0
    N_B = N_A + 2 * KA
    N_P1 = N_B + 3 * KB
    N_P2 = N_P1 + 2 * KD
    N_WO = N_P2 + 2 * KD
    N_F = N_WO + KD
    G = KF // 2
    X_A, Y_A = 0, NT // 2
    X_B, Y_B = X_A + KA, Y_A + KA
    X_P1, Y_P1 = X_B + 3 * KB // 2, Y_B + 3 * KB // 2
    X_P2, Y_P2 = X_P1 + KD, Y_P1 + KD
    X_WO, Y_WO = X_P2 + KD, Y_P2 + KD
    X_F0, Y_F0 = X_WO + KD // 2, Y_WO + KD // 2
    X_F1, Y_F1 = X_F0 + 2, Y_F0 + 2
    X_DL, Y_DL = X_F1 + 6 * (G - 1), Y_F1 + 6 * (G - 1)
    X_END, Y_END = X_DL + KD // 2, Y_DL + KD // 2
    S_MEAN = 1 + (NT + 1) // 2
    S_VAR = S_MEAN + 2
    S_LNR = S_VAR + 1
    S_XT = S_LNR + 2
    S_STATE = S_XT + NT
    S_MS = S_STATE + 1
    S_R2 = S_MS + 1
    S_FST = S_R2 + 2
    S_END = S_FST + 1
    SKIP = (NT + 1) // 2
    Q_F = KB + 2 * KA

    PACKS = [
        [("dw_a", TAPS_A * KA), ("b_dw_a", KA)],
        [("cache_conv_a", HA * KA), ("cache_conv_b", H * KB)],
        [("dw_f", TAPS_F * KF), ("cache_ffn_conv", H * KF), ("dw_b", TAPS_B * KB), ("ln_a_g", KA)],
        [("ln_a_b", KA), ("b_gate", 2 * KD), ("norm2_g", KD)],
    ]
    C, pack_rows, n = {}, [], 0
    for pack in PACKS:
        pack_rows.append(sum(r for _, r in pack))
        assert pack_rows[-1] <= P and n % 2 == 0
        for name, rows in pack:
            C[name] = n
            n += rows
    NC = n
    pack_at = [C[p[0][0]] for p in PACKS]

    at = [-(-nc.sbuf_base // 64) * 64]

    def place(name, shape, dtype, offset=None):
        size = 4
        for s in shape[1:]:
            size *= s
        if offset is None:
            offset = at[0]
            at[0] += -(-size // 64) * 64
            assert at[0] <= nc.sbuf_usable_end
        return nc.alloc_sbuf_tensor_at(name, shape, dtype, offset=offset), offset

    h_hi, _ = place("h_hi", [P, KD, W], F32R)
    h_lo, _ = place("h_lo", [P, KD, W], F32R)
    q_hi, _ = place("q_hi", [P, KA, W], F32R)
    q_lo, _ = place("q_lo", [P, KA, W], F32R)
    mid, mid_at = place("mid", [P, KD * W], F32)
    res, _ = place("res", [P, KD * W], F32)
    w_raw, _ = place("w_raw", [P, 2, KD * P], F32)
    w_hi, _ = place("w_hi", [P, 2, KD * P], F32R)
    w_lo, _ = place("w_lo", [P, 2, KD * P], F32R)
    t0, _ = place("t0", [P, W], F32)
    t1, _ = place("t1", [P, W], F32)
    xr, _ = place("xr", [P, 3 * D], F32)
    cols, _ = place("cols", [P, NC], F32)
    ident, _ = place("ident", [P, P], F32)
    ones, _ = place("ones", [P, P], F32)
    state, _ = place("state", [P, 2 * H * (KB + KF) + 2 * HA * KA], F32)
    state_rows, _ = place("state_rows", [P, 4, P], F32)
    stats, _ = place("stats", [P, 64], F32)
    U_AT = KD * W - KA * UW
    u_in = mid[:, U_AT:].rearrange("p (c n) -> p c n", c=KA)
    merged = mid[:, :].rearrange("p (c n) -> p c n", c=KD)
    XHAT = 4
    assert XHAT * D <= U_AT
    wd_raw = mid[:, 0:2 * D]
    wd_hi, _ = place("wd_hi", [P, 2, D], F32R, mid_at + 4 * 2 * D)
    wd_lo, _ = place("wd_lo", [P, 2, D], F32R, mid_at + 4 * 4 * D)
    rb2 = mid[:, 6 * D:6 * D + W]
    gf_row = mid[:, 6 * D + SW:7 * D + SW]
    assert 7 * D + SW <= KD * W
    cv = res[:, 0:KA * CVW].rearrange("p (c n) -> p c n", c=KA)
    EA = KA * CVW
    EB = EA + CVW
    EC = EB + SW
    bw_in, v_row, e_b, e_c = res[:, EA:EA + W], res[:, EB:EB + W], res[:, EB:EB + SW], res[:, EC:EC + SW]
    assert EC + SW <= KD * W and SW >= CVW
    packs = res[:, 0:4 * P].rearrange("p (k n) -> p k n", k=4)
    g1_row = res[:, EB:EB + D]
    stream = res[:, :].rearrange("p (c n) -> p c n", c=KD)
    x_slot = [xr[:, s * D:(s + 1) * D] for s in range(3)]
    sq = [xr[:, 0:CVW], xr[:, SW:SW + CVW]]
    diag = xr[:, SW:2 * SW]
    sq2 = xr[:, 0:SW]
    sl, ac = xr[:, 0:W], xr[:, W:2 * W]
    ss, ms, rs = stats[:, 0:NT], stats[:, NT:2 * NT], stats[:, 2 * NT:3 * NT]
    m9, r9 = stats[:, 3 * NT:4 * NT], stats[:, 4 * NT:5 * NT]
    half = stats[:, 5 * NT:6 * NT]
    ST_B = 2 * HA * KA
    ST_F = ST_B + 2 * H * KB

    def out_rows(t):
        return mid[:, t * D:(t + 1) * D] if t < 6 else xr[:, (t - 6) * D:(t - 5) * D]

    def every(ap, first, count, step, k):
        return ap[:, first:first + count * step].rearrange("p (r c) -> p r c", c=step)[:, :, bass.ds(k, 1)]

    def col(name, k):
        return cols[:, bass.ds(C[name] + k, 1)]

    with ExitStack() as ctx:
        X = ctx.enter_context(nc.psum_tensor("X", [P, CHUNKS, 512], F32))
        Y = ctx.enter_context(nc.psum_tensor("Y", [P, CHUNKS, 512], F32))
        S = ctx.enter_context(nc.psum_tensor("S", [P, 2, 512], F32))
        S_flat = S[:, :, :].rearrange("p b n -> p (b n)")

        def sem(name):
            return ctx.enter_context(nc.semaphore(name))

        x_in = [sem(f"x_in{s}") for s in range(3)]
        xr_in = [sem(f"xr_in{s}") for s in range(2)]
        params_in, g1_in, gf_in = sem("params_in"), sem("g1_in"), sem("gf_in")
        w_in = [sem("w_in0"), sem("w_in1")]
        wd_in = sem("wd_in")
        stored = sem("stored")
        x_out, y_out, s_out = sem("x_out"), sem("y_out"), sem("s_out")
        unit_done, down_done, s_full, xt_done = sem("unit_done"), sem("down_done"), sem("s_full"), sem("xt_done")
        whi_done, wlo_done = sem("whi_done"), sem("wlo_done")
        wdhi_done, wdlo_done = sem("wdhi_done"), sem("wdlo_done")
        hhi_done, hlo_done = sem("hhi_done"), sem("hlo_done")
        qhi_done, qlo_done = sem("qhi_done"), sem("qlo_done")
        const_done, mean_done, rs_done, pads_done = sem("const_done"), sem("mean_done"), sem("rs_done"), sem("pads_done")
        ss_done, sq_done, silu_done, state_done = sem("ss_done"), sem("sq_done"), sem("silu_done"), sem("state_done")
        xhat_done, hist_done, u_part, tap_done = sem("xhat_done"), sem("hist_done"), sem("u_part"), sem("tap_done")
        b_step, ln_step, prod_done, stat_step = sem("b_step"), sem("ln_step"), sem("prod_done"), sem("stat_step")
        f_step, y_done = sem("f_step"), sem("y_done")

        def rows3(ap):
            return ap.rearrange("p (c n) -> p c n", c=CHUNKS)

        def bank(b):
            return b[:, :, 0:CW]

        B_STEPS = 5
        F_STEPS = 6

        w_in_cols = ins["w_in"].rearrange("l (k p) c -> p (l k) c", p=P)
        w_a_cols = ins["w_a_out"].rearrange("l (k p) c -> p (l k) c", p=P)
        w_b_cols = ins["w_b_out"].rearrange("l (k p) c -> p (l k) c", p=P)
        w_o_cols = ins["w_o"].rearrange("l (k p) c -> p (l k) c", p=P)
        w_up_cols = ins["w_up"].rearrange("l (k p) c -> p (l k) c", p=P)
        w_down_rows = ins["w_down"].rearrange("l (g k p) c -> (l g) p k c", p=P, k=2)
        x_rows = [ins["x_prompt"].rearrange("b s d -> (b s) d"), ins["x_sample"].rearrange("b s d -> (b s) d")]
        y_rows = [outs["y_prompt"].rearrange("b s d -> (b s) d"), outs["y_sample"].rearrange("b s d -> (b s) d")]
        AG, AV = DA, 0
        BG, BC, BV = 2 * DA, 2 * DA + DB, 2 * DA + 2 * DB
        GA = 2 * DA + 3 * DB
        GB = GA + D

        block = ctx.enter_context(nc.Block())

        @block.sync
        def _(sp):
            def x_load(t):
                g, r, rows, _ = TILES[t]
                if t >= 3:
                    sp.wait_ge(xhat_done, t - 2)
                    sp.wait_ge(ss_done, t - 2)
                sp.dma_start(x_slot[t % 3][0:rows, :], x_rows[g][r:r + rows, :]).then_inc(x_in[t % 3], 16)

            def load(src, c, n0, per=0, i=0, first=False):
                s, k = n0 % 2, src.shape[1]
                if not first:
                    n = n0 + per * i
                    sp.wait_ge(wlo_done, n - 1)
                sp.dma_start(w_raw[:, s, 0:k * P].rearrange("p (k c) -> p k c", k=k),
                             src[:, :, bass.ds(c, P)]).then_inc(w_in[s], 16)

            for t in range(3):
                x_load(t)
            sp.dma_start(g1_row, ins["norm1_g"][0:1, :].to_broadcast([P, D])).then_inc(g1_in, 16)
            load(w_in_cols, AG, 0, first=True)
            load(w_in_cols, AV, 1, first=True)
            for t in range(3, NT):
                x_load(t)
            with sp.Fori(2, KA + 1) as j:
                load(w_in_cols, AG - P + P * j, N_A - 2, 2, j)
                load(w_in_cols, AV - P + P * j, N_A - 1, 2, j)
            with sp.Fori(0, KB // 2) as b:
                for u in range(2):
                    load(w_in_cols, BC + P * (2 * b + u), N_B + 3 * u, 6, b)
                    load(w_in_cols, BV + P * (2 * b + u), N_B + 3 * u + 1, 6, b)
                    load(w_in_cols, BG + P * (2 * b + u), N_B + 3 * u + 2, 6, b)
            for n0, gate, proj in ((N_P1, GB, w_b_cols), (N_P2, GA, w_a_cols)):
                with sp.Fori(1, KD // 2 + 1) as i:
                    load(w_in_cols, gate - 2 * P + 2 * P * i, n0 - 4, 4, i)
                    load(w_in_cols, gate - P + 2 * P * i, n0 - 3, 4, i)
                    load(proj, 2 * P * i - 2 * P, n0 - 2, 4, i)
                    load(proj, 2 * P * i - P, n0 - 1, 4, i)
            with sp.Fori(0, KD // 2) as i:
                load(w_o_cols, 2 * P * i, N_WO, 2, i)
                load(w_o_cols, 2 * P * i + P, N_WO + 1, 2, i)
            with sp.Fori(0, G) as i:
                load(w_up_cols, 2 * P * i, N_F, 4, i)
                load(w_up_cols, DF + 2 * P * i, N_F + 1, 4, i)
                load(w_up_cols, 2 * P * i + P, N_F + 2, 4, i)
                load(w_up_cols, DF + 2 * P * i + P, N_F + 3, 4, i)
                sp.wait_ge(hlo_done, KD)
                sp.dma_start(wd_raw.rearrange("p (k c) -> p k c", k=2),
                             w_down_rows[bass.ds(i, 1), :, :, :].rearrange("g p k c -> p (g k) c")
                             ).then_inc(wd_in, 16)
            sp.dma_start(gf_row, ins["final_g"].rearrange("(a d) -> a d", a=1).to_broadcast([P, D])).then_inc(gf_in, 16)
            n_out = 0
            sp.wait_ge(s_out, S_STATE + 1)
            for s, group in enumerate(("p", "s")):
                sp.dma_start(outs[f"new_conv_a_{group}"].rearrange("l b r (c p) -> (l b r c) p", p=P),
                             state_rows[0:HA * KA, s, :]).then_inc(stored, 16)
                sp.dma_start(outs[f"new_conv_b_{group}"].rearrange("l b r (c p) -> (l b r c) p", p=P),
                             state_rows[s * H * KB:(s + 1) * H * KB, 2, :]).then_inc(stored, 16)
            sp.wait_ge(s_out, S_FST + 1)
            for s, group in enumerate(("p", "s")):
                sp.dma_start(outs[f"new_ffn_conv_{group}"].rearrange("l b r (c p) -> (l b r c) p", p=P),
                             state_rows[s * H * KF:(s + 1) * H * KF, 3, :]).then_inc(stored, 16)
            for t, (g, r, rows, _) in enumerate(TILES):
                sp.wait_ge(y_done, t + 1)
                sp.dma_start(y_rows[g][r:r + rows, :], out_rows(t)[0:rows, :]).then_inc(stored, 16)
            sp.wait_ge(stored, 16 * (6 + NT))

        @block.gpsimd
        def _(pool):
            pool.memset(ident[:, :], 0.0).then_inc(const_done, 1)
            pool.wait_ge(const_done, 1)
            pool.affine_select(out=ident[:, :], in_=ident[:, :], compare_op=ALU.not_equal, fill=1.0, base=0,
                               pattern=[[-1, P]], channel_multiplier=1).then_inc(const_done, 1)
            pool.memset(half, -0.5).then_inc(const_done, 1)
            pool.memset(ones[:, :], 1.0).then_inc(const_done, 1)
            for part in (h_hi, h_lo):
                for c in (0, S0 - H):
                    pool.memset(part[:, :, c:c + H].bitcast(F32), 0.0).then_inc(const_done, 1)
            for part in (q_hi, q_lo):
                pool.memset(part[:, :, 0:H].bitcast(F32), 0.0).then_inc(const_done, 1)
            pool.memset(u_in[:, :, 0:HA - H], 0.0).then_inc(const_done, 1)

            def rms_of_rows(t, rows, base):
                pool.wait_ge(ss_done, base + t + 1)
                pool.tensor_scalar(ms[0:rows, t:t + 1], ss[0:rows, t:t + 1], 1.0 / D, RMS_EPS,
                                   ALU.mult, ALU.add).then_inc(mean_done, 1)
                pool.wait_ge(mean_done, base + t + 1)
                pool.tensor_tensor(rs[0:rows, t:t + 1], ms[0:rows, t:t + 1], half[0:rows, 0:1],
                                   ALU.pow).then_inc(rs_done, 1)

            for t, (_, _, rows, _) in enumerate(TILES):
                rms_of_rows(t, rows, 0)
            pool.wait_ge(b_step, B_STEPS * KB)
            pool.memset(e_b[:, CVW:SW], 0.0).then_inc(pads_done, 1)
            pool.wait_ge(s_out, S_VAR + 1)
            pool.tensor_tensor(r9, m9, half, ALU.pow).then_inc(rs_done, 1)
            pool.wait_ge(qlo_done, KB + 2 * KA)
            for c in (0, S0 - H):
                pool.memset(stream[:, :, c:c + H], 0.0).then_inc(pads_done, 1)
            pool.wait_ge(s_full, S_XT + NT - SKIP)
            pool.memset(sq2, 0.0).then_inc(stat_step, 1)
            pool.wait_ge(s_out, S_MS + 1)
            pool.tensor_tensor(r9, m9, half, ALU.pow).then_inc(rs_done, 1)
            for t, (_, _, rows, _) in enumerate(TILES):
                pool.wait_ge(ss_done, NT + t + 1)
                pool.tensor_scalar(ms[0:rows, t:t + 1], ss[0:rows, t:t + 1], 1.0 / D, RMS_EPS,
                                   ALU.mult, ALU.add).then_inc(mean_done, 1)
                pool.wait_ge(mean_done, NT + t + 1)
                pool.tensor_tensor(rs[0:rows, t:t + 1], ms[0:rows, t:t + 1], half[0:rows, 0:1],
                                   ALU.pow).then_inc(rs_done, 1)

        @block.tensor
        def _(pe):
            def chunk(dst, c, slot, k_tiles, hi, lo, before=None, whi=w_hi, wlo=w_lo, wcol=None):
                for k in range(k_tiles):
                    if before:
                        before(k)
                    for p, (w, a) in enumerate(((whi, hi), (whi, lo), (wlo, hi))):
                        lhs = w[:, slot, k * P:(k + 1) * P] if wcol is None else w[:, k, wcol:wcol + P]
                        last = pe.matmul(dst[:, c, 0:CW], lhs, a[:, k, c * CW:(c + 1) * CW],
                                         start=(k == 0 and p == 0), stop=(k == k_tiles - 1 and p == 2))
                return last

            def unit(n0, per, i, free, uses, k_tiles, hi, lo, hooks=(), before=None):
                slot = n0 % 2
                b = (X, Y)[slot]
                pe.wait_ge(wlo_done, n0 + 1 + per * i)
                pe.wait_ge(free, uses)
                for c in range(CHUNKS):
                    last = chunk(b, c, slot, k_tiles, hi, lo, before=before and before(c))
                    if c == CHUNKS - 1:
                        last.then_inc(unit_done, 1)
                    if c < len(hooks) and hooks[c]:
                        hooks[c]()

            pe.wait_ge(const_done, 2)
            pe.wait_ge(params_in, 16 * sum(len(p) for p in PACKS))
            for k, rows in enumerate(pack_rows):
                last = pe.transpose(S[:, 0, pack_at[k]:pack_at[k] + rows], packs[0:rows, k, :], ident[0:rows, 0:rows])
            last.then_inc(s_full, 1)

            def turn_input(t):
                rows = TILES[t][2]
                pe.wait_ge(xhat_done, t + 1)
                b, free, uses = (Y, y_out, t // 2) if t % 2 else (S, s_out, 1 + t // 2)
                pe.wait_ge(free, uses)
                for k in range(KD):
                    last = pe.transpose(b[:, k // 4, (k % 4) * P:(k % 4) * P + rows],
                                        mid[0:rows, (t % XHAT) * D + k * P:(t % XHAT) * D + (k + 1) * P],
                                        ident[0:rows, 0:rows])
                last.then_inc(xt_done, 1)

            def turned(t):
                pe.wait_ge(s_out, 2 + t // 2)
                if t:
                    pe.wait_ge(y_out, (t + 1) // 2)

            need = [max(t for t, tile in enumerate(TILES) if tile[3] < (c + 1) * CW) for c in range(CHUNKS)]
            done = need[0] + 3
            pe.wait_ge(const_done, 11)
            for t in range(done):
                turn_input(t)

            def between(lo, hi):
                def run():
                    for t in range(lo, hi):
                        turn_input(t)
                return run

            def when_turned(c):
                return lambda k: turned(need[c]) if k == 0 else None

            unit(N_A, 0, 0, x_out, 0, KD, h_hi, h_lo, before=when_turned,
                 hooks=(between(done, min(done + 3, NT)), between(min(done + 3, NT), NT)))
            unit(N_A + 1, 0, 0, y_out, Y_A, KD, h_hi, h_lo)
            with pe.Fori(1, KA) as j:
                unit(N_A, 2, j, x_out, X_A + j, KD, h_hi, h_lo)
                unit(N_A + 1, 2, j, y_out, Y_A + j, KD, h_hi, h_lo)
            with pe.Fori(0, KB // 2) as b:
                unit(N_B, 6, b, x_out, X_B + 3 * b, KD, h_hi, h_lo)
                unit(N_B + 1, 6, b, y_out, Y_B + 3 * b, KD, h_hi, h_lo)
                unit(N_B + 2, 6, b, x_out, X_B + 1 + 3 * b, KD, h_hi, h_lo)
                unit(N_B + 3, 6, b, y_out, Y_B + 1 + 3 * b, KD, h_hi, h_lo)
                unit(N_B + 4, 6, b, x_out, X_B + 2 + 3 * b, KD, h_hi, h_lo)
                unit(N_B + 5, 6, b, y_out, Y_B + 2 + 3 * b, KD, h_hi, h_lo)

            def row_of(src, part):
                def run():
                    if part == 0:
                        for c in range(2):
                            last = pe.matmul(S[:, c, :], ones[:, :], src[:, c * 512:(c + 1) * 512], start=True, stop=True)
                    else:
                        last = pe.matmul(S[:, 0, 0:SW - 1024], ones[:, :], src[:, 1024:SW], start=True, stop=True)
                    last.then_inc(s_full, 1)
                return run

            def mean_row(part):
                def run():
                    if part == 0:
                        pe.wait_ge(ln_step, 3)
                        pe.wait_ge(pads_done, 1)
                    pe.wait_ge(s_out, S_MEAN + part)
                    row_of(e_b, part)()
                return run

            def sum_columns(src):
                for t in range(NT):
                    last = pe.matmul(S[:, 0, t:t + 1], src[:, t * P:(t + 1) * P], ones[:, 0:1], start=True, stop=True)
                last.then_inc(s_full, 1)

            def ln_columns():
                pe.wait_ge(ln_step, 10)
                pe.wait_ge(s_out, S_VAR)
                sum_columns(e_b)

            def ln_row(part):
                def run():
                    if part == 0:
                        pe.wait_ge(ln_step, 11)
                    pe.wait_ge(s_out, S_LNR + part)
                    row_of(diag, part)()
                return run

            def mix_pair(n0, xb, yb, i, q_need, hooks=((), (), (), ())):
                unit(n0, 4, i, x_out, xb + 2 * i, KD, h_hi, h_lo, hooks[0])
                unit(n0 + 1, 4, i, y_out, yb + 2 * i, KD, h_hi, h_lo, hooks[1])
                pe.wait_ge(qlo_done, q_need)
                unit(n0 + 2, 4, i, x_out, xb + 1 + 2 * i, KB, q_hi, q_lo, hooks[2])
                unit(n0 + 3, 4, i, y_out, yb + 1 + 2 * i, KB, q_hi, q_lo, hooks[3])

            with pe.Fori(0, KD // 2 - 1) as i:
                mix_pair(N_P1, X_P1, Y_P1, i, KB)
            mix_pair(N_P1, X_P1, Y_P1, KD // 2 - 1, KB,
                     ((None, None, mean_row(0)), (mean_row(1),), (None, None, ln_columns), (None, ln_row(0), ln_row(1))))

            def turn_residual(t, use, loads, s):
                rows = TILES[t][2] if isinstance(t, int) else P
                pe.wait_ge(xr_in[s], 16 * loads)
                pe.wait_ge(s_out, use)
                for k in range(KD):
                    last = pe.transpose(S[:, k // 4, (k % 4) * P:(k % 4) * P + rows],
                                        xr[0:rows, s * D + k * P:s * D + (k + 1) * P], ident[0:rows, 0:rows])
                last.then_inc(s_full, 1)

            with pe.Fori(0, KD // 2) as i:
                mix_pair(N_P2, X_P2, Y_P2, i, KB + 2 * KA,
                         ((), (), (None, None, lambda: turn_residual(None, S_XT + 2 * i, i + 1, 0)),
                          (None, None, lambda: turn_residual(None, S_XT + 1 + 2 * i, i + 1, 1))))
            turn_residual(NT - 1, S_XT + NT - 1, KD // 2 + 1, 0)

            def merged_ready(c):
                return (lambda k: pe.wait_ge(hlo_done, k + 1)) if c == 0 else None

            with pe.Fori(0, KD // 2) as i:
                unit(N_WO, 2, i, x_out, X_WO + i, KD, h_hi, h_lo, before=merged_ready)
                unit(N_WO + 1, 2, i, y_out, Y_WO + i, KD, h_hi, h_lo)

            pe.wait_ge(state_done, 2)
            pe.wait_ge(b_step, B_STEPS * KB)
            pe.wait_ge(s_out, S_STATE)
            for s in range(2):
                pe.transpose(S[0:HA * KA, 0, s * P:(s + 1) * P], state[:, s * HA * KA:(s + 1) * HA * KA], ident[:, :])
            pe.transpose(S[0:2 * H * KB, 0, 2 * P:3 * P], state[:, ST_B:ST_F], ident[:, :]).then_inc(s_full, 1)

            def ffn_in(c):
                return lambda k: pe.wait_ge(hlo_done, KD + KD * c + k + 1)

            def rms_columns():
                pe.wait_ge(stat_step, 1 + KD)
                pe.wait_ge(s_out, S_MS)
                sum_columns(sq2)

            def rms_row(part):
                def run():
                    if part == 0:
                        pe.wait_ge(stat_step, KD + 2)
                    pe.wait_ge(s_out, S_R2 + part)
                    row_of(diag, part)()
                return run

            unit(N_F, 0, 0, x_out, X_F0, KD, h_hi, h_lo, (None, None, rms_columns), before=ffn_in)
            unit(N_F + 1, 0, 0, y_out, Y_F0, KD, h_hi, h_lo, (None, rms_row(0), rms_row(1)))
            unit(N_F + 2, 0, 0, x_out, X_F0 + 1, KD, h_hi, h_lo)
            unit(N_F + 3, 0, 0, y_out, Y_F0 + 1, KD, h_hi, h_lo)

            def down(group, x_use, y_use):
                pe.wait_ge(wdlo_done, group + 1)
                pe.wait_ge(qlo_done, KB + 2 * KA + 2 * group + 2)
                for m in range(KD):
                    b, free, uses = ((Y, y_out, y_use), (X, x_out, x_use))[m % 2]
                    pe.wait_ge(free, uses + m // 2)
                    for c in range(CHUNKS):
                        last = chunk(b, c, 0, 2, q_hi, q_lo, whi=wd_hi, wlo=wd_lo, wcol=m * P)
                    last.then_inc(down_done, 1)

            with pe.Fori(1, G) as i:
                xb, yb = X_F1 - 6 + 6 * i, Y_F1 - 6 + 6 * i
                unit(N_F, 4, i, x_out, xb, KD, h_hi, h_lo)
                down(i - 1, xb + 1, yb)
                unit(N_F + 1, 4, i, y_out, yb + 4, KD, h_hi, h_lo)
                unit(N_F + 2, 4, i, x_out, xb + 5, KD, h_hi, h_lo)
                unit(N_F + 3, 4, i, y_out, yb + 5, KD, h_hi, h_lo)
            down(G - 1, X_DL, Y_DL)

            pe.wait_ge(f_step, F_STEPS * KF)
            pe.wait_ge(x_out, X_END)
            pe.wait_ge(y_out, Y_END)
            pe.wait_ge(s_out, S_FST)
            pe.transpose(S[0:2 * H * KF, 0, 0:P], state[:, ST_F:], ident[:, :]).then_inc(s_full, 1)
            for t, (_, _, rows, c0) in enumerate(TILES):
                b = (X, Y, S)[t % 3]
                if t >= 3:
                    pe.wait_ge(y_done, t - 2)
                if t == 2:
                    pe.wait_ge(s_out, S_END)
                for k in range(KD):
                    last = pe.transpose(b[0:rows, k // 4, (k % 4) * P:(k % 4 + 1) * P],
                                        stream[:, k, c0:c0 + rows], ident[:, :])
                last.then_inc(xt_done, 1)

        @block.scalar
        def _(act):
            for k, pack in enumerate(PACKS):
                r = 0
                for name, rows in pack:
                    src = ins[name]
                    dims = " ".join("abcd"[:len(src.shape) - 1])
                    src = src.rearrange(f"{dims} (k p) -> ({dims} k) p", p=P)
                    act.dma_start(packs[r:r + rows, k, :], src).then_inc(params_in, 16)
                    r += rows

            def split_hi(n0, per=0, i=0, k_tiles=KD, first=False):
                s = n0 % 2
                act.wait_ge(w_in[s], 16 * (n0 // 2 + 1) + 16 * (per // 2) * i)
                if not first:
                    act.wait_ge(unit_done, n0 - 1 + per * i)
                act.activation(w_hi[:, s, 0:k_tiles * P], w_raw[:, s, 0:k_tiles * P], ACT.Copy).then_inc(whi_done, 1)

            def square_rows(t):
                rows = TILES[t][2]
                act.wait_ge(x_in[t % 3], 16 * (t // 3 + 1))
                if t:
                    act.wait_ge(ss_done, t)
                act.activation(t1[0:rows, 0:D], x_slot[t % 3][0:rows, :], ACT.Square,
                               accum_out=ss[0:rows, t:t + 1]).then_inc(ss_done, 1)

            square_rows(0)
            square_rows(1)
            act.wait_ge(s_full, 1)
            act.activation(cols[:, :], S[:, 0, 0:NC], ACT.Copy).then_inc(s_out, 1)
            split_hi(0, first=True)
            split_hi(1, first=True)
            for t, (_, _, rows, c0) in enumerate(TILES):
                if t + 2 < NT:
                    square_rows(t + 2)
                act.wait_ge(xt_done, t + 1)
                b = Y if t % 2 else S
                act.activation(h_hi[:, :, c0:c0 + rows],
                               b[:, 0:2, :].rearrange("p b (k n) -> p (b k) n", n=P)[:, :, 0:rows],
                               ACT.Copy).then_inc(hhi_done, 1)

            def sigmoid(b, dst, bias, n, out):
                act.wait_ge(unit_done, n + 1)
                act.activation(rows3(dst), bank(b), ACT.Sigmoid, bias=bias).then_inc(out, 1)

            with act.Fori(0, KA) as j:
                split_hi(N_A + 2, 2, j)
                act.wait_ge(y_out, Y_A + j)
                sigmoid(X, t0[:, :], 0.0, N_A + 2 * j, x_out)
                split_hi(N_A + 3, 2, j)
            act.wait_ge(y_out, Y_A + KA)
            for s, c0 in enumerate((HA + NP - HA, UW - HA)):
                act.activation(state[:, s * HA * KA:(s + 1) * HA * KA].rearrange("p (r c) -> p c r", c=KA),
                               u_in[:, :, c0:c0 + HA], ACT.Copy).then_inc(state_done, 1)
            with act.Fori(0, KB // 2) as b:
                for u in range(2):
                    bk, out = ((X, x_out), (Y, y_out))[u]
                    nb = N_B + 3 * u
                    split_hi(nb + 2, 6, b)
                    act.wait_ge(*((x_out, X_B + 3 * b), (y_out, Y_B + 3 * b + 1))[u])
                    act.wait_ge(unit_done, nb + 1 + 6 * b)
                    act.activation(rows3(t0[:, :]), bank(bk), ACT.Copy).then_inc(out, 1)
                    split_hi(nb + 3, 6, b)
                    split_hi(nb + 4, 6, b, k_tiles=KD)
                    use = (X_B + 3 * b + 2, Y_B + 3 * b + 3)[u]
                    act.wait_ge((x_out, y_out)[u], use)
                    act.activation(q_hi[:, bass.ds(2 * b + u, 1), H:W], t1[:, H:W].rearrange("p (a n) -> p a n", a=1),
                                   ACT.Copy).then_inc(qhi_done, 1)

            def mix_gates(n0, gate, i, temps_free):
                for u in range(2):
                    split_hi(n0 + 2 + u, 4, i, k_tiles=KB)
                    temps_free(u)
                    sigmoid((X, Y)[u], (t0, t1)[u][:, :], col("b_gate", gate + u + 2 * i), n0 + u + 4 * i,
                            (x_out, y_out)[u])

            def mix_tail(n0, i):
                split_hi(n0 + 4, 4, i)
                split_hi(n0 + 5, 4, i)

            def b_free(i):
                def run(u):
                    act.wait_ge((x_out, y_out)[u], (X_P1, Y_P1)[u] + 2 * i)
                    if u:
                        act.wait_ge(qlo_done, KB)
                return run

            with act.Fori(0, KD // 2 - 1) as i:
                mix_gates(N_P1, KD, i, b_free(i))
                mix_tail(N_P1, i)
            i = KD // 2 - 1

            def copy_row(dst, n, part, scale=1.0, width=CVW):
                act.wait_ge(s_full, n + 1 + part - SKIP)
                lo, hi = (0, 1024) if part == 0 else (1024, width)
                act.activation(dst[:, lo:hi], S_flat[:, 0:hi - lo], ACT.Copy, scale=scale).then_inc(s_out, 1)

            b_free(i)(0)
            split_hi(N_P1 + 2, 4, i, k_tiles=KB)
            sigmoid(X, t0[:, :], col("b_gate", KD + 2 * i), N_P1 + 4 * i, x_out)
            copy_row(e_c, S_MEAN, 0, 1.0 / DA)
            copy_row(e_c, S_MEAN, 1, 1.0 / DA)
            for c in range(KA):
                act.wait_ge(ln_step, 3 + c + 1)
                if c >= 2:
                    act.wait_ge(ln_step, 3 + KA + c - 1)
                act.activation(sq[c % 2], cv[:, c, :], ACT.Square).then_inc(sq_done, 1)
            split_hi(N_P1 + 3, 4, i, k_tiles=KB)
            b_free(i)(1)
            sigmoid(Y, t1[:, :], col("b_gate", KD + 1 + 2 * i), N_P1 + 1 + 4 * i, y_out)
            mix_tail(N_P1, i)
            copy_row(e_c, S_LNR, 0)
            copy_row(e_c, S_LNR, 1)
            act.wait_ge(unit_done, N_P2)
            for c in range(KA):
                act.wait_ge(ln_step, 11 + c + 1)
                act.activation(cv[:, c, :], cv[:, c, :], ACT.Silu, scale=col("ln_a_g", c),
                               bias=col("ln_a_b", c)).then_inc(silu_done, 1)
            for c in range(KA):
                act.wait_ge(silu_done, c + 1)
                for a, b, n in ((0, P0, NP), (CS, S0, NS)):
                    act.activation(q_hi[:, c, b:b + n], cv[:, c, a:a + n], ACT.Copy).then_inc(qhi_done, 1)

            def a_free(i):
                def run(u):
                    act.wait_ge(wlo_done, N_P2 + 3 + 4 * i)
                    act.wait_ge((x_out, y_out)[u], (X_P2, Y_P2)[u] + 2 * i)
                return run

            def load_x(t, s, turned_before):
                act.wait_ge(s_full, turned_before)
                act.dma_start(xr[:, s * D:(s + 1) * D], x_rows[0][bass.ds(t * P, P), :]).then_inc(xr_in[s], 16)

            def residual(t, c0, rows, use):
                act.wait_ge(s_full, use + 1 - SKIP)
                act.wait_ge(qlo_done, KB + 2 * KA)
                act.activation(stream[:, :, bass.ds(c0, rows)],
                               S[:, :, :].rearrange("p b (k n) -> p (b k) n", n=P)[:, :, 0:rows],
                               ACT.Copy).then_inc(s_out, 1)

            def merged_hi(k):
                act.wait_ge(prod_done, k + 1)
                act.activation(h_hi[:, k, :], merged[:, k, :], ACT.Copy).then_inc(hhi_done, 1)

            def merge_pair(i, early=(), late=((), ())):
                load_x(2 * i, 0, S_XT - SKIP + 2 * i)
                load_x(2 * i + 1, 1, S_XT - SKIP + 2 * i)
                mix_gates(N_P2, 0, i, a_free(i))
                for k in early:
                    merged_hi(k)
                for u in range(2):
                    for k in late[u]:
                        merged_hi(k)
                    split_hi(N_P2 + 4 + u, 4, i)
                    residual(2 * i + u, P0 + (2 * i + u) * P, P, S_XT + 2 * i + u)

            with act.Fori(0, KD // 2 - 1) as i:
                merge_pair(i)
            merge_pair(KD // 2 - 1, range(KD - 2), ((KD - 2,), (KD - 1,)))
            act.wait_ge(s_full, S_XT - SKIP + NT - 1)
            act.dma_start(xr[0:NS, 0:D], x_rows[1][0:NS, :]).then_inc(xr_in[0], 16)
            residual(NT - 1, S0, NS, S_XT + NT - 1)
            with act.Fori(0, KD // 2) as i:
                for u in range(2):
                    split_hi(N_WO + 2 + u, 2, i)
                    act.wait_ge((x_out, y_out)[u], (X_WO, Y_WO)[u] + i + 1)
                    act.activation((t0, t1)[u][:, :], res[:, bass.ds((2 * i + u) * W, W)],
                                   ACT.Square).then_inc(sq_done, 1)
            act.wait_ge(unit_done, N_F)
            act.wait_ge(y_out, Y_F0)
            act.wait_ge(x_out, X_F0)
            for c in range(CHUNKS):
                for k in range(KD):
                    act.activation(h_hi[:, k, c * CW:(c + 1) * CW], stream[:, k, c * CW:(c + 1) * CW], ACT.Copy,
                                   scale=col("norm2_g", k)).then_inc(hhi_done, 1)
            act.wait_ge(s_full, S_STATE + 1 - SKIP)
            act.activation(state_rows[0:HA * KA, 0:2, :].rearrange("p a n -> p (a n)"), S[0:HA * KA, 0, 0:2 * P],
                           ACT.Copy).then_inc(state_done, 1)
            act.activation(state_rows[0:2 * H * KB, 2, :], S[0:2 * H * KB, 0, 2 * P:3 * P], ACT.Copy).then_inc(s_out, 1)

            def silu(f):
                act.wait_ge(f_step, F_STEPS * f + 5)
                act.activation(sl, t1[:, :], ACT.Silu).then_inc(silu_done, 1)

            def ffn_hi(f, u, out, use):
                act.wait_ge(out, use)
                act.activation(q_hi[:, u, :], ac, ACT.Copy).then_inc(qhi_done, 1)

            def split_down(g):
                act.wait_ge(wd_in, 16 * g + 16)
                act.wait_ge(down_done, KD * g)
                act.activation(wd_hi[:, :, :].rearrange("p k c -> p (k c)"), wd_raw, ACT.Copy).then_inc(wdhi_done, 1)

            split_hi(N_F + 2)
            copy_row(rb2, S_R2, 0, 1.0, W)
            copy_row(rb2, S_R2, 1, 1.0, W)
            silu(0)
            split_hi(N_F + 3)
            split_down(0)
            ffn_hi(0, 0, y_out, Y_F0 + 1)
            split_hi(N_F + 4)
            silu(1)
            split_hi(N_F + 5)
            ffn_hi(1, 1, y_out, Y_F0 + 2)
            with act.Fori(1, G - 1) as i:
                yb = Y_F1 - 6 + 6 * i
                split_hi(N_F + 2, 4, i)
                silu(2 * i)
                split_hi(N_F + 3, 4, i)
                split_down(i)
                ffn_hi(2 * i, 0, y_out, yb + 5)
                split_hi(N_F + 4, 4, i)
                silu(2 * i + 1)
                split_hi(N_F + 5, 4, i)
                ffn_hi(2 * i + 1, 1, y_out, yb + 6)
            i = G - 1
            yb = Y_F1 - 6 + 6 * i
            split_hi(N_F + 2, 4, i)
            silu(2 * i)
            split_hi(N_F + 3, 4, i)
            split_down(i)
            ffn_hi(2 * i, 0, y_out, yb + 5)
            silu(2 * i + 1)
            ffn_hi(2 * i + 1, 1, y_out, yb + 6)
            act.wait_ge(s_full, S_FST + 1 - SKIP)
            act.activation(state_rows[0:2 * H * KF, 3, :], S[0:2 * H * KF, 0, 0:P], ACT.Copy).then_inc(s_out, 1)
            for t, (_, _, rows, _) in enumerate(TILES):
                b = (X, Y, S)[t % 3]
                act.wait_ge(xt_done, NT + t + 1)
                act.wait_ge(ss_done, NT + t)
                act.activation(t0[0:rows, 0:D], b[0:rows, 0:2, :].rearrange("p b n -> p (b n)"), ACT.Square,
                               accum_out=ss[0:rows, t:t + 1]).then_inc(ss_done, 1)

        @block.vector
        def _(dve):
            def sub(out, full, hi, done):
                dve.tensor_tensor(out, full, hi.bitcast(F32), ALU.subtract).then_inc(done, 1)

            def split_lo(n0, per=0, i=0, k_tiles=KD):
                s, n = n0 % 2, k_tiles * P
                dve.wait_ge(whi_done, n0 + 1 + per * i)
                sub(w_lo[:, s, 0:n], w_raw[:, s, 0:n], w_hi[:, s, 0:n], wlo_done)

            def normalise(t):
                rows = TILES[t][2]
                dve.wait_ge(rs_done, t + 1)
                if t >= XHAT:
                    dve.wait_ge(xt_done, t - XHAT + 1)
                dve.scalar_tensor_tensor(mid[0:rows, (t % XHAT) * D:(t % XHAT + 1) * D], x_slot[t % 3][0:rows, :],
                                         rs[0:rows, t:t + 1], g1_row[0:rows, :], ALU.mult,
                                         ALU.mult).then_inc(xhat_done, 1)

            dve.wait_ge(g1_in, 16)
            normalise(0)
            normalise(1)
            split_lo(0)
            for t, (_, _, rows, c0) in enumerate(TILES):
                if t + 2 < NT:
                    normalise(t + 2)
                dve.wait_ge(hhi_done, t + 1)
                b, out = (Y, y_out) if t % 2 else (S, s_out)
                sub(h_lo[:, :, c0:c0 + rows], b[:, 0:2, :].rearrange("p b (k n) -> p (b k) n", n=P)[:, :, 0:rows],
                    h_hi[:, :, c0:c0 + rows], out)
                if t == 2:
                    split_lo(1)
            dve.wait_ge(const_done, 11)
            dve.tensor_copy(u_in[:, :, US - HA:US],
                            cols[:, C["cache_conv_a"]:C["cache_conv_a"] + HA * KA].rearrange("p (r c) -> p c r", c=KA)
                            ).then_inc(hist_done, 1)
            dve.memset(res[:, EB:EB + H], 0.0).then_inc(hist_done, 1)

            def first_tap(c):
                dve.wait_ge(hist_done, 2)
                dve.tensor_scalar(res[:, bass.ds(c * CVW, CVW)], mid[:, bass.ds(U_AT + c * UW, CVW)],
                                  col("dw_a", c), col("b_dw_a", c), ALU.mult, ALU.add).then_inc(tap_done, 1)

            def tap(c, k):
                dve.wait_ge(tap_done, c * TAPS_A + k)
                dst = res[:, bass.ds(c * CVW, CVW)]
                dve.scalar_tensor_tensor(dst, mid[:, bass.ds(U_AT + c * UW + k, CVW)], col("dw_a", k * KA + c), dst,
                                         ALU.mult, ALU.add).then_inc(tap_done, 1)

            def glu(j):
                dve.wait_ge(x_out, X_A + j + 1)
                dve.wait_ge(unit_done, N_A + 2 * j + 2)
                base = U_AT + j * UW + HA - H
                cut = (CHUNKS - 1) * CW
                end = S0 - H - cut
                dve.tensor_tensor(mid[:, bass.ds(base, cut)].rearrange("p (c n) -> p c n", c=CHUNKS - 1),
                                  Y[:, 0:CHUNKS - 1, 0:CW],
                                  t0[:, 0:cut].rearrange("p (c n) -> p c n", c=CHUNKS - 1), ALU.mult).then_inc(u_part, 1)
                dve.tensor_tensor(mid[:, bass.ds(base + cut, end)], Y[:, CHUNKS - 1, 0:end], t0[:, cut:cut + end],
                                  ALU.mult).then_inc(u_part, 1)
                dve.tensor_tensor(mid[:, bass.ds(U_AT + j * UW + US, NS)], Y[:, CHUNKS - 1, CW - NS:CW], t0[:, S0:W],
                                  ALU.mult).then_inc(y_out, 1)

            split_lo(N_A + 2)
            glu(0)
            split_lo(N_A + 3)
            dve.wait_ge(y_out, Y_A + 1)
            first_tap(0)
            per = (TAPS_A - 1) // (KA - 1)
            with dve.Fori(1, KA) as j:
                for r in range(per // 2):
                    tap(0, 1 - per + r + per * j)
                split_lo(N_A + 2, 2, j)
                for r in range(per // 2, per):
                    tap(0, 1 - per + r + per * j)
                glu(j)
                split_lo(N_A + 3, 2, j)

            def mixer_b(b, u, taps):
                nb, c = N_B + 3 * u, 2 * b + u
                val, val_out, gate, gate_out = ((Y, y_out, X, x_out), (X, x_out, Y, y_out))[u]
                c_out, c_use = ((x_out, X_B + 3 * b + 1), (y_out, Y_B + 3 * b + 2))[u]
                v_use = (Y_B + 3 * b + 1, X_B + 3 * b + 3)[u]
                step = B_STEPS * u + 2 * B_STEPS * b
                split_lo(nb + 2, 6, b)
                taps(3 * u)
                dve.wait_ge(c_out, c_use)
                dve.wait_ge(unit_done, nb + 2 + 6 * b)
                dve.tensor_tensor(rows3(bw_in), bank(val), rows3(t0[:, :]), ALU.mult).then_inc(val_out, 1)
                split_lo(nb + 3, 6, b)
                dve.wait_ge(val_out, v_use)
                dve.tensor_copy(bw_in[:, S0 - H:S0].rearrange("p (r a) -> p r a", a=1),
                                every(cols, C["cache_conv_b"], H, KB, c)).then_inc(b_step, 1)
                for s, c0 in enumerate((P0 + NP - H, W - H)):
                    st = dve.tensor_copy(every(state, ST_B + s * H * KB, H, KB, c),
                                         bw_in[:, c0:c0 + H].rearrange("p (r a) -> p r a", a=1))
                st.then_inc(b_step, 1)
                dve.wait_ge(b_step, step + 1)
                out = v_row[:, H:W]
                dve.tensor_scalar(out, bw_in[:, 0:W - H], col("dw_b", c), None, ALU.mult).then_inc(b_step, 1)
                for k in range(1, TAPS_B):
                    dve.wait_ge(b_step, step + 2 + k)
                    dve.scalar_tensor_tensor(out, bw_in[:, k:k + W - H], col("dw_b", k * KB + c), out,
                                             ALU.mult, ALU.add).then_inc(b_step, 1)
                taps(3 * u + 1)
                split_lo(nb + 4, 6, b)
                dve.wait_ge(b_step, step + B_STEPS)
                dve.wait_ge(unit_done, nb + 3 + 6 * b)
                dve.tensor_tensor(rows3(t1[:, :]), bank(gate), rows3(v_row), ALU.mult).then_inc(gate_out, 1)
                taps(3 * u + 2)
                dve.wait_ge(qhi_done, c + 1)
                sub(q_lo[:, bass.ds(c, 1), H:W], t1[:, H:W].rearrange("p (a n) -> p a n", a=1),
                    q_hi[:, bass.ds(c, 1), H:W], qlo_done)

            dve.wait_ge(y_out, Y_A + KA)
            per6 = (TAPS_A - 1) // 6
            with dve.Fori(0, KB // 2) as b:
                first_tap(b + 1)

                def taps(place):
                    for k in range(1 + per6 * place, 1 + per6 * (place + 1)):
                        tap(b + 1, k)

                for u in range(2):
                    mixer_b(b, u, taps)

            def merge_b(m0, u, i, n):
                bk, out = ((X, x_out), (Y, y_out))[u]
                dve.wait_ge(unit_done, n + 1)
                dve.wait_ge(out, (X_P1, Y_P1)[u] + 1 + 2 * i)
                dve.tensor_tensor(mid[:, bass.ds((2 * i + u) * W, W)].rearrange("p (c n) -> p c n", c=CHUNKS),
                                  bank(bk), rows3((t0, t1)[u][:, :]), ALU.mult).then_inc(out, 1)

            first_tap(KA - 1)
            with dve.Fori(0, KD // 2 - 1) as i:
                k = 0
                for u, taps_here in ((0, 3), (1, 3), (2, 2), (3, 2)):
                    split_lo(N_P1 + 2 + u, 4, i, k_tiles=KB if u < 2 else KD)
                    if u >= 2:
                        merge_b(0, u - 2, i, N_P1 + u + 4 * i)
                    for _ in range(taps_here):
                        tap(KA - 1, 1 + k + per * i)
                        k += 1
            i = KD // 2 - 1
            dve.wait_ge(tap_done, KA * TAPS_A)
            dve.tensor_tensor(e_b[:, 0:CVW], cv[:, 0, :], cv[:, 1, :], ALU.add).then_inc(ln_step, 1)
            for c in range(2, KA):
                dve.wait_ge(ln_step, c - 1)
                dve.tensor_tensor(e_b[:, 0:CVW], e_b[:, 0:CVW], cv[:, c, :], ALU.add).then_inc(ln_step, 1)
            split_lo(N_P1 + 2, 4, i, k_tiles=KB)
            dve.wait_ge(s_out, S_MEAN + 2)
            for c in range(KA):
                dve.tensor_tensor(cv[:, c, :], cv[:, c, :], e_c[:, 0:CVW], ALU.subtract).then_inc(ln_step, 1)
            dve.wait_ge(sq_done, 2)
            dve.tensor_tensor(e_b[:, 0:CVW], sq[0], sq[1], ALU.add).then_inc(ln_step, 1)
            for c in range(2, KA):
                dve.wait_ge(sq_done, c + 1)
                dve.wait_ge(ln_step, 3 + KA + c - 1)
                dve.tensor_tensor(e_b[:, 0:CVW], e_b[:, 0:CVW], sq[c % 2], ALU.add).then_inc(ln_step, 1)
            split_lo(N_P1 + 3, 4, i, k_tiles=KB)
            split_lo(N_P1 + 4, 4, i)
            merge_b(0, 0, i, N_P1 + 2 + 4 * i)

            def moments(use, n, eps):
                dve.wait_ge(s_full, use + 1 - SKIP)
                dve.tensor_scalar(m9, S[:, 0, 0:NT], 1.0 / n, eps, ALU.mult, ALU.add).then_inc(s_out, 1)

            def diagonals(done, count):
                dve.wait_ge(rs_done, count)
                dve.tensor_tensor(diag.rearrange("p (t n) -> p t n", t=NT),
                                  ident[:, :].rearrange("p (a n) -> p a n", a=1).to_broadcast([P, NT, P]),
                                  r9.rearrange("p (t a) -> p t a", a=1).to_broadcast([P, NT, P]),
                                  ALU.mult).then_inc(done, 1)

            moments(S_VAR, DA, LN_EPS)
            diagonals(ln_step, NT + 1)
            split_lo(N_P1 + 5, 4, i)
            merge_b(0, 1, i, N_P1 + 3 + 4 * i)
            dve.wait_ge(s_out, S_LNR + 2)
            for c in range(KA):
                dve.tensor_tensor(cv[:, c, :], cv[:, c, :], e_c[:, 0:CVW], ALU.mult).then_inc(ln_step, 1)
            for c in range(KA):
                for u, (a, b, n) in enumerate(((0, P0, NP), (CS, S0, NS))):
                    dve.wait_ge(qhi_done, KB + 2 * c + u + 1)
                    sub(q_lo[:, c, b:b + n], cv[:, c, a:a + n], q_hi[:, c, b:b + n], qlo_done)

            def merge_a(u, i):
                bk, out = ((X, x_out), (Y, y_out))[u]
                t = (t0, t1)[u]
                dve.wait_ge(out, (X_P2, Y_P2)[u] + 1 + 2 * i)
                dve.wait_ge(unit_done, N_P2 + 3 + u + 4 * i)
                dve.tensor_tensor(rows3(t[:, :]), bank(bk), rows3(t[:, :]), ALU.mult).then_inc(out, 1)
                dve.wait_ge(out, (X_P2, Y_P2)[u] + 2 + 2 * i)
                m = mid[:, bass.ds((2 * i + u) * W, W)]
                dve.tensor_tensor(m, m, t[:, :], ALU.add).then_inc(prod_done, 1)

            def merged_lo(k):
                dve.wait_ge(hhi_done, NT + k + 1)
                sub(h_lo[:, k, :], merged[:, k, :], h_hi[:, k, :], hlo_done)

            with dve.Fori(0, KD // 2 - 1) as i:
                for u in range(4):
                    split_lo(N_P2 + 2 + u, 4, i, k_tiles=KB if u < 2 else KD)
                    if u >= 2:
                        merge_a(u - 2, i)
            i = KD // 2 - 1
            split_lo(N_P2 + 2, 4, i, k_tiles=KB)
            split_lo(N_P2 + 3, 4, i, k_tiles=KB)
            for k in range(KD - 2):
                merged_lo(k)
            for u in range(2):
                merge_a(u, i)
                merged_lo(KD - 2 + u)
                split_lo(N_P2 + 4 + u, 4, i)

            dve.wait_ge(s_out, S_XT + NT)
            dve.wait_ge(pads_done, 3)
            with dve.Fori(0, KD // 2) as i:
                for u in range(2):
                    bk, out, use = ((X, x_out, X_WO), (Y, y_out, Y_WO))[u]
                    split_lo(N_WO + 2 + u, 2, i)
                    dve.wait_ge(unit_done, N_WO + 1 + u + 2 * i)
                    x = res[:, bass.ds((2 * i + u) * W, W)]
                    dve.tensor_tensor(x.rearrange("p (c n) -> p c n", c=CHUNKS), bank(bk),
                                      x.rearrange("p (c n) -> p c n", c=CHUNKS), ALU.add).then_inc(out, 1)
                    dve.wait_ge(sq_done, KA + 1 + u + 2 * i)
                    dve.wait_ge(stat_step, 1 + u + 2 * i)
                    dve.tensor_tensor(sq2[:, 0:W], sq2[:, 0:W], (t0, t1)[u][:, :], ALU.add).then_inc(stat_step, 1)
            for c in range(CHUNKS):
                for k in range(KD):
                    dve.wait_ge(hhi_done, NT + KD + c * KD + k + 1)
                    dve.scalar_tensor_tensor(h_lo[:, k, c * CW:(c + 1) * CW], stream[:, k, c * CW:(c + 1) * CW],
                                             col("norm2_g", k), h_hi[:, k, c * CW:(c + 1) * CW].bitcast(F32),
                                             ALU.mult, ALU.subtract).then_inc(hlo_done, 1)
            moments(S_MS, D, RMS_EPS)
            diagonals(stat_step, NT + 2)

            def gate(f, n, use):
                dve.wait_ge(unit_done, n + 1)
                dve.tensor_tensor(rows3(t0[:, :]), bank(X), rows3(rb2), ALU.mult).then_inc(x_out, 1)
                dve.wait_ge(x_out, use + 1)
                dve.tensor_copy(t0[:, S0 - H:S0].rearrange("p (r a) -> p r a", a=1),
                                every(cols, C["cache_ffn_conv"], H, KF, f)).then_inc(f_step, 1)
                for s, c0 in enumerate((P0 + NP - H, W - H)):
                    st = dve.tensor_copy(every(state, ST_F + s * H * KF, H, KF, f),
                                         t0[:, c0:c0 + H].rearrange("p (r a) -> p r a", a=1))
                st.then_inc(f_step, 1)

            def conv(f, k):
                out = t1[:, H:W]
                dve.wait_ge(f_step, F_STEPS * f + (1 if k == 0 else 2 + k))
                if k == 0:
                    dve.tensor_scalar(out, t0[:, 0:W - H], col("dw_f", f), None, ALU.mult).then_inc(f_step, 1)
                else:
                    dve.scalar_tensor_tensor(out, t0[:, k:k + W - H], col("dw_f", k * KF + f), out,
                                             ALU.mult, ALU.add).then_inc(f_step, 1)

            def scale_silu(f):
                dve.wait_ge(silu_done, KA + 1 + f)
                dve.tensor_tensor(sl, sl, rb2, ALU.mult).then_inc(f_step, 1)

            def value(f, n):
                dve.wait_ge(f_step, F_STEPS * f + F_STEPS)
                dve.wait_ge(unit_done, n + 1)
                dve.tensor_tensor(rows3(ac), bank(Y), rows3(sl), ALU.mult).then_inc(y_out, 1)

            def ffn_lo(f, u):
                dve.wait_ge(qhi_done, Q_F + f + 1)
                sub(q_lo[:, u, :], ac, q_hi[:, u, :], qlo_done)

            def split_down(g):
                dve.wait_ge(wdhi_done, g + 1)
                sub(wd_lo[:, :, :].rearrange("p k c -> p (k c)"), wd_raw,
                    wd_hi[:, :, :].rearrange("p k c -> p (k c)"), wdlo_done)

            def add_down(g, m):
                bk, out = ((Y, y_out), (X, x_out))[m % 2]
                dve.wait_ge(down_done, KD * g + m + 1)
                x = rows3(stream[:, m, :])
                dve.tensor_tensor(x, bank(bk), x, ALU.add).then_inc(out, 1)

            split_lo(N_F + 2)
            dve.wait_ge(s_out, S_R2 + 2)
            gate(0, N_F, X_F0)
            for k in range(TAPS_F):
                conv(0, k)
            split_lo(N_F + 3)
            scale_silu(0)
            value(0, N_F + 1)
            split_down(0)
            ffn_lo(0, 0)
            split_lo(N_F + 4)
            gate(1, N_F + 2, X_F0 + 1)
            for k in range(TAPS_F):
                conv(1, k)
            split_lo(N_F + 5)
            scale_silu(1)
            value(1, N_F + 3)
            ffn_lo(1, 1)

            def ffn_group(i, more):
                xb = X_F1 - 6 + 6 * i
                gate(2 * i, N_F + 4 * i, xb)
                split_lo(N_F + 2, 4, i)
                conv(2 * i, 0)
                for m in range(KD):
                    add_down(i - 1, m)
                    if m + 1 < TAPS_F:
                        conv(2 * i, m + 1)
                    if m == 4:
                        scale_silu(2 * i)
                split_lo(N_F + 3, 4, i)
                split_down(i)
                value(2 * i, N_F + 1 + 4 * i)
                ffn_lo(2 * i, 0)
                if more:
                    split_lo(N_F + 4, 4, i)
                gate(2 * i + 1, N_F + 2 + 4 * i, xb + 5)
                for k in range(TAPS_F):
                    conv(2 * i + 1, k)
                if more:
                    split_lo(N_F + 5, 4, i)
                scale_silu(2 * i + 1)
                value(2 * i + 1, N_F + 3 + 4 * i)
                ffn_lo(2 * i + 1, 1)

            with dve.Fori(1, G - 1) as i:
                ffn_group(i, True)
            ffn_group(G - 1, False)
            for m in range(KD):
                add_down(G - 1, m)

            dve.wait_ge(gf_in, 16)
            for t, (_, _, rows, _) in enumerate(TILES):
                b = (X, Y, S)[t % 3]
                dve.wait_ge(rs_done, NT + 2 + t + 1)
                dve.scalar_tensor_tensor(out_rows(t)[0:rows, :], b[0:rows, 0:2, :].rearrange("p b n -> p (b n)"),
                                         rs[0:rows, t:t + 1], gf_row[0:rows, :], ALU.mult, ALU.mult).then_inc(y_done, 1)


_INS = ["x_prompt", "x_sample", "cache_conv_a", "cache_conv_b", "cache_ffn_conv", "norm1_g", "w_in", "b_gate",
        "dw_a", "b_dw_a", "ln_a_g", "ln_a_b", "w_a_out", "dw_b", "w_b_out", "w_o", "norm2_g", "w_up", "dw_f",
        "w_down", "final_g"]
_OUTS = ["y_prompt", "y_sample", "new_conv_a_p", "new_conv_b_p", "new_ffn_conv_p",
         "new_conv_a_s", "new_conv_b_s", "new_ffn_conv_s"]


def kernel(**inputs):
    import concourse.bacc as bacc
    import numpy as np
    from concourse.bass_utils import run_bass_kernel_spmd

    nc = bacc.Bacc("TRN2", target_bir_lowering=False, num_devices=1, dynamic_dma_scratch_size=1024)
    arrays = {f"in_{n}": np.ascontiguousarray(inputs[n]) for n in _INS}
    shapes = {
        "y_prompt": inputs["x_prompt"].shape,
        "y_sample": inputs["x_sample"].shape,
    }
    for name in ("conv_a", "conv_b", "ffn_conv"):
        depth, batch, rows, width = inputs[f"cache_{name}"].shape
        shapes[f"new_{name}_p"] = (depth, inputs["x_prompt"].shape[0], rows, width)
        shapes[f"new_{name}_s"] = (depth, batch, rows, width)
    ins = {n: nc.dram_tensor(f"in_{n}", arrays[f"in_{n}"].shape, F32, kind="ExternalInput").ap() for n in _INS}
    outs = {n: nc.dram_tensor(f"out_{n}", shapes[n], F32, kind="ExternalOutput").ap() for n in _OUTS}
    streaming_encoder(nc, ins, outs)
    got = run_bass_kernel_spmd(nc, [arrays], core_ids=[0])
    return tuple(got.results[0][f"out_{n}"] for n in _OUTS)
```

```python
from contextlib import ExitStack

import concourse.bass as bass
from concourse import mybir

F32 = mybir.dt.float32
F32R = mybir.dt.float32r
ALU = mybir.AluOpType
ACT = mybir.ActivationFunctionType

P = 128
CHUNKS = 3


def streaming_encoder(nc: bass.Bass, ins, outs):
    D = ins["x_prompt"].shape[2]
    NP = ins["x_prompt"].shape[1]
    NS = ins["x_sample"].shape[1]
    TAPS_A, DA = ins["dw_a"].shape[1:]
    TAPS_B, DB = ins["dw_b"].shape[1:]
    TAPS_F, DF = ins["dw_f"].shape[1:]
    RMS_EPS, LN_EPS = 1e-6, 1e-5
    KD, KA, KB, KF = D // P, DA // P, DB // P, DF // P
    HA, H = TAPS_A - 1, TAPS_B - 1
    assert TAPS_F == TAPS_B == 3 and KA == KB == 4 and KD == 8 and KF % 2 == 0

    P0 = H
    S0 = 2 * H + NP
    W = S0 + NS
    CW = W // CHUNKS
    assert CW * CHUNKS == W and CW % 2 == 0 and CW <= 512
    UW = 2 * HA + NP + NS
    CVW = UW - HA
    US = 2 * HA + NP
    CS = HA + NP
    TILES = [(0, r, P, P0 + r) for r in range(0, NP, P)] + [(1, 0, NS, S0)]
    NT = len(TILES)
    SW = NT * P

    T3 = NT // CHUNKS
    CUTS = [0] + [P0 + T3 * P * c for c in range(1, CHUNKS)] + [W]
    CUT_LEN = [b - a for a, b in zip(CUTS, CUTS[1:])]
    assert T3 * CHUNKS == NT and 256 <= min(CUT_LEN) and max(CUT_LEN) <= 512

    N_A = 0
    N_B = N_A + 2 * KA
    N_P1 = N_B + 3 * KB
    N_P2 = N_P1 + 2 * KD
    N_WO = N_P2 + 2 * KD
    N_F = N_WO + KD
    G = KF // 2
    X_A, Y_A = 0, NT // 2
    X_B, Y_B = X_A + KA, Y_A + KA
    X_P1, Y_P1 = X_B + 3 * KB // 2, Y_B + 3 * KB // 2
    X_P2, Y_P2 = X_P1 + KD, Y_P1 + KD
    X_WO, Y_WO = X_P2 + KD, Y_P2 + KD
    X_F0, Y_F0 = X_WO + KD // 2, Y_WO + KD // 2
    X_F1, Y_F1 = X_F0 + 2, Y_F0 + 2
    X_DL = X_F1 + 6 * (G - 1)
    S_COLS = (NT + 1) // 2
    S_MEAN = S_COLS + 1
    S_VAR = S_MEAN + 2
    S_LNR = S_VAR + 1
    S_XT = S_LNR + 2
    S_STATE = S_XT + NT
    S_MS = S_STATE + 1
    S_R2 = S_MS + 1
    S_FST = S_R2 + 2
    S_END = S_FST + 1
    SKIP = (NT + 1) // 2
    Q_F = KB + 2 * KA

    PACKS = [
        [("dw_a", TAPS_A * KA), ("b_dw_a", KA)],
        [("cache_conv_a", HA * KA), ("cache_conv_b", H * KB)],
        [("dw_f", TAPS_F * KF), ("cache_ffn_conv", H * KF), ("dw_b", TAPS_B * KB), ("ln_a_g", KA)],
        [("ln_a_b", KA), ("b_gate", 2 * KD), ("norm2_g", KD)],
    ]
    C, pack_rows, n = {}, [], 0
    for pack in PACKS:
        pack_rows.append(sum(r for _, r in pack))
        assert pack_rows[-1] <= P and n % 2 == 0
        for name, rows in pack:
            C[name] = n
            n += rows
    NC = n
    pack_at = [C[p[0][0]] for p in PACKS]

    at = [-(-nc.sbuf_base // 64) * 64]

    def place(name, shape, dtype, offset=None):
        size = 4
        for s in shape[1:]:
            size *= s
        if offset is None:
            offset = at[0]
            at[0] += -(-size // 64) * 64
            assert at[0] <= nc.sbuf_usable_end
        return nc.alloc_sbuf_tensor_at(name, shape, dtype, offset=offset), offset

    h_hi, h_at = place("h_hi", [P, KD, W], F32R)
    h_lo, _ = place("h_lo", [P, KD, W], F32R)
    q_hi, _ = place("q_hi", [P, KA, W], F32R)
    q_lo, _ = place("q_lo", [P, KA, W], F32R)
    mid, mid_at = place("mid", [P, KD * W], F32)
    res, _ = place("res", [P, KD * W], F32)
    w_raw, _ = place("w_raw", [P, 2, KD * P], F32)
    w_hi, _ = place("w_hi", [P, 2, KD * P], F32R)
    w_lo, _ = place("w_lo", [P, 2, KD * P], F32R)
    t0, _ = place("t0", [P, W], F32)
    t1, _ = place("t1", [P, W], F32)
    xr, _ = place("xr", [P, 3 * D], F32)
    cols, _ = place("cols", [P, NC], F32)
    ident, _ = place("ident", [P, P], F32)
    ones, _ = place("ones", [P, P], F32)
    state, _ = place("state", [P, 2 * H * (KB + KF) + 2 * HA * KA], F32)
    state_rows, _ = place("state_rows", [P, 4, P], F32)
    stats, _ = place("stats", [P, 64], F32)
    U_AT = KD * W - KA * UW
    u_in = mid[:, U_AT:].rearrange("p (c n) -> p c n", c=KA)
    merged = mid[:, :].rearrange("p (c n) -> p c n", c=KD)
    XHAT = 4
    assert XHAT * D <= U_AT
    wd_raw = mid[:, 0:2 * D]
    wd_hi, _ = place("wd_hi", [P, 2, D], F32R, mid_at + 4 * 2 * D)
    wd_lo, _ = place("wd_lo", [P, 2, D], F32R, mid_at + 4 * 4 * D)
    rb2 = mid[:, 6 * D:6 * D + W]
    gf_row = mid[:, 6 * D + SW:7 * D + SW]
    assert 7 * D + SW <= KD * W
    out_rows, _ = place("out_rows", [P, NT, D], F32, h_at)
    cv = res[:, 0:KA * CVW].rearrange("p (c n) -> p c n", c=KA)
    EA = KA * CVW
    EB = EA + CVW
    EC = EB + SW
    bw_in, v_row, e_b, e_c = res[:, EA:EA + W], res[:, EB:EB + W], res[:, EB:EB + SW], res[:, EC:EC + SW]
    assert EC + SW <= KD * W and SW >= CVW
    packs = res[:, 0:4 * P].rearrange("p (k n) -> p k n", k=4)
    g1_row = res[:, EB:EB + D]
    stream = res[:, :].rearrange("p (c n) -> p c n", c=KD)
    x_slot = [xr[:, s * D:(s + 1) * D] for s in range(3)]
    sq = [xr[:, 0:CVW], xr[:, SW:SW + CVW]]
    diag = xr[:, SW:2 * SW]
    sq2 = xr[:, 0:SW]
    sl, ac = xr[:, 0:W], xr[:, W:2 * W]
    ss, ms, rs = stats[:, 0:NT], stats[:, NT:2 * NT], stats[:, 2 * NT:3 * NT]
    m9, r9 = stats[:, 3 * NT:4 * NT], stats[:, 4 * NT:5 * NT]
    half = stats[:, 5 * NT:6 * NT]
    ST_B = 2 * HA * KA
    ST_F = ST_B + 2 * H * KB


    def every(ap, first, count, step, k):
        return ap[:, first:first + count * step].rearrange("p (r c) -> p r c", c=step)[:, :, bass.ds(k, 1)]

    def col(name, k):
        return cols[:, bass.ds(C[name] + k, 1)]

    with ExitStack() as ctx:
        X = ctx.enter_context(nc.psum_tensor("X", [P, CHUNKS, 512], F32))
        Y = ctx.enter_context(nc.psum_tensor("Y", [P, CHUNKS, 512], F32))
        S = ctx.enter_context(nc.psum_tensor("S", [P, 2, 512], F32))
        S_flat = S[:, :, :].rearrange("p b n -> p (b n)")

        def sem(name):
            return ctx.enter_context(nc.semaphore(name))

        x_in = [sem(f"x_in{s}") for s in range(3)]
        xr_in = [sem(f"xr_in{s}") for s in range(2)]
        params_in, g1_in, gf_in = sem("params_in"), sem("g1_in"), sem("gf_in")
        w_in = [sem("w_in0"), sem("w_in1")]
        wd_in = sem("wd_in")
        stored = sem("stored")
        x_out, y_out, s_out = sem("x_out"), sem("y_out"), sem("s_out")
        unit_done, down_done, s_full, xt_done = sem("unit_done"), sem("down_done"), sem("s_full"), sem("xt_done")
        whi_done, wlo_done = sem("whi_done"), sem("wlo_done")
        wdhi_done, wdlo_done = sem("wdhi_done"), sem("wdlo_done")
        hhi_done, hlo_done = sem("hhi_done"), sem("hlo_done")
        qhi_done, qlo_done = sem("qhi_done"), sem("qlo_done")
        const_done, mean_done, rs_done, pads_done = sem("const_done"), sem("mean_done"), sem("rs_done"), sem("pads_done")
        warm = sem("warm")
        ss_done, sq_done, silu_done, state_done = sem("ss_done"), sem("sq_done"), sem("silu_done"), sem("state_done")
        xhat_done, hist_done, u_part, tap_done = sem("xhat_done"), sem("hist_done"), sem("u_part"), sem("tap_done")
        b_step, ln_step, prod_done, stat_step = sem("b_step"), sem("ln_step"), sem("prod_done"), sem("stat_step")
        f_step, y_done = sem("f_step"), sem("y_done")
        wo_part, added_part = sem("wo_part"), sem("added_part")
        value_part, ac_part, qhi_part, qlo_part = sem("value_part"), sem("ac_part"), sem("qhi_part"), sem("qlo_part")
        last_added = sem("last_added")

        def last_wo(c):
            return (wo_part, c + 1) if c < CHUNKS - 1 else (unit_done, N_F)

        def last_wo_added(c):
            return (added_part, c + 1) if c < CHUNKS - 1 else (y_out, Y_F0)

        LAST_BANKS = 4
        TURN_BEFORE = [(1, 1), (1, 3), (1, 7), (2, 1), (2, 4), (2, 6)]
        NORM_AFTER = [(1, 4), (1, 6), (2, 2), (2, 4)]

        def rows3(ap):
            return ap.rearrange("p (c n) -> p c n", c=CHUNKS)

        def bank(b):
            return b[:, :, 0:CW]

        B_STEPS = 5
        F_STEPS = 6

        OUT_BANKS = [((S, 0), (Y, 1))[t % 2] for t in range(NT - T3)] + [(X, 0), (S, 0), (Y, 1)]

        def input_banks(t, rows):
            b = Y[:, 1:3, :] if t % 2 else S[:, :, :]
            return b.rearrange("p b (k n) -> p (b k) n", n=P)[:, :, 0:rows]

        def output_banks(t):
            b, first_bank = OUT_BANKS[t]
            return b[0:TILES[t][2], first_bank:first_bank + 2, :].rearrange("p b n -> p (b n)")

        w_in_cols = ins["w_in"].rearrange("l (k p) c -> p (l k) c", p=P)
        w_a_cols = ins["w_a_out"].rearrange("l (k p) c -> p (l k) c", p=P)
        w_b_cols = ins["w_b_out"].rearrange("l (k p) c -> p (l k) c", p=P)
        w_o_cols = ins["w_o"].rearrange("l (k p) c -> p (l k) c", p=P)
        w_up_cols = ins["w_up"].rearrange("l (k p) c -> p (l k) c", p=P)
        w_down_rows = ins["w_down"].rearrange("l (g k p) c -> (l g) p k c", p=P, k=2)
        x_rows = [ins["x_prompt"].rearrange("b s d -> (b s) d"), ins["x_sample"].rearrange("b s d -> (b s) d")]
        y_rows = [outs["y_prompt"].rearrange("b s d -> (b s) d"), outs["y_sample"].rearrange("b s d -> (b s) d")]
        AG, AV = DA, 0
        BG, BC, BV = 2 * DA, 2 * DA + DB, 2 * DA + 2 * DB
        GA = 2 * DA + 3 * DB
        GB = GA + D

        block = ctx.enter_context(nc.Block())

        @block.sync
        def _(sp):
            def x_load(t):
                g, r, rows, _ = TILES[t]
                if t >= 3:
                    sp.wait_ge(xhat_done, t - 2)
                    sp.wait_ge(ss_done, t - 2)
                sp.dma_start(x_slot[t % 3][0:rows, :], x_rows[g][r:r + rows, :]).then_inc(x_in[t % 3], 16)

            def load(src, c, n0, per=0, i=0, first=False):
                s, k = n0 % 2, src.shape[1]
                if not first:
                    n = n0 + per * i
                    sp.wait_ge(wlo_done, n - 1)
                sp.dma_start(w_raw[:, s, 0:k * P].rearrange("p (k c) -> p k c", k=k),
                             src[:, :, bass.ds(c, P)]).then_inc(w_in[s], 16)

            x_load(0)
            sp.dma_start(g1_row, ins["norm1_g"][0:1, :].to_broadcast([P, D])).then_inc(g1_in, 16)
            x_load(1)
            x_load(2)
            load(w_in_cols, AG, 0, first=True)
            x_load(3)
            load(w_in_cols, AV, 1, first=True)
            for t in range(4, NT):
                x_load(t)
            for k, pack in enumerate(PACKS):
                r = 0
                for name, rows in pack:
                    src = ins[name]
                    dims = " ".join("abcd"[:len(src.shape) - 1])
                    src = src.rearrange(f"{dims} (k p) -> ({dims} k) p", p=P)
                    sp.dma_start(packs[r:r + rows, k, :], src).then_inc(params_in, 16)
                    r += rows
            with sp.Fori(2, KA + 1) as j:
                load(w_in_cols, AG - P + P * j, N_A - 2, 2, j)
                load(w_in_cols, AV - P + P * j, N_A - 1, 2, j)
            with sp.Fori(0, KB // 2) as b:
                for u in range(2):
                    load(w_in_cols, BC + P * (2 * b + u), N_B + 3 * u, 6, b)
                    load(w_in_cols, BV + P * (2 * b + u), N_B + 3 * u + 1, 6, b)
                    load(w_in_cols, BG + P * (2 * b + u), N_B + 3 * u + 2, 6, b)
            for n0, gate, proj in ((N_P1, GB, w_b_cols), (N_P2, GA, w_a_cols)):
                with sp.Fori(1, KD // 2 + 1) as i:
                    load(w_in_cols, gate - 2 * P + 2 * P * i, n0 - 4, 4, i)
                    load(w_in_cols, gate - P + 2 * P * i, n0 - 3, 4, i)
                    load(proj, 2 * P * i - 2 * P, n0 - 2, 4, i)
                    load(proj, 2 * P * i - P, n0 - 1, 4, i)
            with sp.Fori(0, KD // 2) as i:
                load(w_o_cols, 2 * P * i, N_WO, 2, i)
                load(w_o_cols, 2 * P * i + P, N_WO + 1, 2, i)
            with sp.Fori(0, G) as i:
                load(w_up_cols, 2 * P * i, N_F, 4, i)
                load(w_up_cols, DF + 2 * P * i, N_F + 1, 4, i)
                load(w_up_cols, 2 * P * i + P, N_F + 2, 4, i)
                load(w_up_cols, DF + 2 * P * i + P, N_F + 3, 4, i)
                sp.wait_ge(hlo_done, KD)
                sp.dma_start(wd_raw.rearrange("p (k c) -> p k c", k=2),
                             w_down_rows[bass.ds(i, 1), :, :, :].rearrange("g p k c -> p (g k) c")
                             ).then_inc(wd_in, 16)
            sp.dma_start(gf_row, ins["final_g"].rearrange("(a d) -> a d", a=1).to_broadcast([P, D])).then_inc(gf_in, 16)
            n_out = 0
            sp.wait_ge(s_out, S_STATE + 1)
            for s, group in enumerate(("p", "s")):
                sp.dma_start(outs[f"new_conv_a_{group}"].rearrange("l b r (c p) -> (l b r c) p", p=P),
                             state_rows[0:HA * KA, s, :]).then_inc(stored, 16)
                sp.dma_start(outs[f"new_conv_b_{group}"].rearrange("l b r (c p) -> (l b r c) p", p=P),
                             state_rows[s * H * KB:(s + 1) * H * KB, 2, :]).then_inc(stored, 16)
            sp.wait_ge(s_out, S_FST + 1)
            for s, group in enumerate(("p", "s")):
                sp.dma_start(outs[f"new_ffn_conv_{group}"].rearrange("l b r (c p) -> (l b r c) p", p=P),
                             state_rows[s * H * KF:(s + 1) * H * KF, 3, :]).then_inc(stored, 16)
            for t, (g, r, rows, _) in enumerate(TILES):
                sp.wait_ge(y_done, t + 1)
                sp.dma_start(y_rows[g][r:r + rows, :], out_rows[0:rows, t, :]).then_inc(stored, 16)
            sp.wait_ge(stored, 16 * (6 + NT))

        @block.gpsimd
        def _(pool):
            pool.memset(ident[:, :], 0.0).then_inc(const_done, 1)
            pool.wait_ge(const_done, 1)
            pool.affine_select(out=ident[:, :], in_=ident[:, :], compare_op=ALU.not_equal, fill=1.0, base=0,
                               pattern=[[-1, P]], channel_multiplier=1).then_inc(const_done, 1)
            pool.memset(half, -0.5).then_inc(const_done, 1)
            pool.memset(ones[:, :], 1.0).then_inc(const_done, 1)
            for part in (h_hi, h_lo):
                for c in (0, S0 - H):
                    pool.memset(part[:, :, c:c + H].bitcast(F32), 0.0).then_inc(const_done, 1)
            for part in (q_hi, q_lo):
                pool.memset(part[:, :, 0:H].bitcast(F32), 0.0).then_inc(const_done, 1)
            pool.memset(u_in[:, :, 0:HA - H], 0.0).then_inc(const_done, 1)

            def rms_of_rows(t, rows, base):
                pool.wait_ge(ss_done, base + t + 1)
                pool.tensor_scalar(ms[0:rows, t:t + 1], ss[0:rows, t:t + 1], 1.0 / D, RMS_EPS,
                                   ALU.mult, ALU.add).then_inc(mean_done, 1)
                pool.wait_ge(mean_done, base + t + 1)
                pool.tensor_tensor(rs[0:rows, t:t + 1], ms[0:rows, t:t + 1], half[0:rows, 0:1],
                                   ALU.pow).then_inc(rs_done, 1)

            for t, (_, _, rows, _) in enumerate(TILES):
                rms_of_rows(t, rows, 0)
            pool.wait_ge(b_step, B_STEPS * KB)
            pool.memset(e_b[:, CVW:SW], 0.0).then_inc(pads_done, 1)
            pool.wait_ge(s_out, S_VAR + 1)
            pool.tensor_tensor(r9, m9, half, ALU.pow).then_inc(rs_done, 1)
            pool.wait_ge(qlo_done, KB + 2 * KA)
            for c in (0, S0 - H):
                pool.memset(stream[:, :, c:c + H], 0.0).then_inc(pads_done, 1)
            pool.wait_ge(s_full, S_XT + NT - SKIP)
            pool.memset(sq2, 0.0).then_inc(stat_step, 1)
            pool.wait_ge(s_out, S_MS + 1)
            pool.tensor_tensor(r9, m9, half, ALU.pow).then_inc(rs_done, 1)
            for t, (_, _, rows, _) in enumerate(TILES):
                pool.wait_ge(ss_done, NT + t + 1)
                pool.tensor_scalar(ms[0:rows, t:t + 1], ss[0:rows, t:t + 1], 1.0 / D, RMS_EPS,
                                   ALU.mult, ALU.add).then_inc(mean_done, 1)
                pool.wait_ge(mean_done, NT + t + 1)
                pool.tensor_tensor(rs[0:rows, t:t + 1], ms[0:rows, t:t + 1], half[0:rows, 0:1],
                                   ALU.pow).then_inc(rs_done, 1)

        @block.tensor
        def _(pe):
            def products(dst, w_at, a, cols, k, first, last):
                hi, lo = a
                for p, (w, act) in enumerate(((w_at[0], hi), (w_at[0], lo), (w_at[1], hi))):
                    done = pe.matmul(dst, w, act[:, k, cols[0]:cols[1]], start=(first and p == 0), stop=(last and p == 2))
                return done

            def unit_weights(slot, k):
                return w_hi[:, slot, k * P:(k + 1) * P], w_lo[:, slot, k * P:(k + 1) * P]

            def third(c):
                return (H if c == 0 else c * CW), (c + 1) * CW

            def chunk(b, c, slot, k_tiles, hi, lo, before=None, cuts=None, pads=False):
                cols = third(c) if cuts is None else (cuts[c], cuts[c + 1])
                if pads:
                    cols = (c * CW, cols[1])
                start = cols[0] - (c * CW if cuts is None else cuts[c])
                for k in range(k_tiles):
                    if before:
                        before(k)
                    last = products(b[:, c, start:start + cols[1] - cols[0]], unit_weights(slot, k), (hi, lo), cols, k,
                                    k == 0, k == k_tiles - 1)
                return last

            def unit(n0, per, i, free, uses, k_tiles, hi, lo, hooks=(), before=None, part=None, cuts=None):
                slot = n0 % 2
                b = (X, Y)[slot]
                pe.wait_ge(wlo_done, n0 + 1 + per * i)
                pe.wait_ge(free, uses)
                for c in range(CHUNKS):
                    last = chunk(b, c, slot, k_tiles, hi, lo, before and before(c), cuts)
                    if c == CHUNKS - 1:
                        last.then_inc(unit_done, 1)
                    elif part:
                        last.then_inc(part, 1)
                    if c < len(hooks) and hooks[c]:
                        hooks[c]()

            def turn_params():
                pe.wait_ge(params_in, 16 * sum(len(p) for p in PACKS))
                pe.wait_ge(s_out, S_COLS)
                for k, rows in enumerate(pack_rows):
                    last = pe.transpose(S[:, 0, pack_at[k]:pack_at[k] + rows], packs[0:rows, k, :],
                                        ident[0:rows, 0:rows])
                last.then_inc(s_full, 1)

            def turn_input(t):
                rows = TILES[t][2]
                pe.wait_ge(xhat_done, t + 1)
                b, first_bank, free = (Y, 1, y_out) if t % 2 else (S, 0, s_out)
                if t >= 2:
                    pe.wait_ge(free, t // 2)
                for k in range(KD):
                    last = pe.transpose(b[:, first_bank + k // 4, (k % 4) * P:(k % 4) * P + rows],
                                        mid[0:rows, (t % XHAT) * D + k * P:(t % XHAT) * D + (k + 1) * P],
                                        ident[0:rows, 0:rows])
                last.then_inc(xt_done, 1)

            def turned(t):
                pe.wait_ge(s_out, 1 + t // 2)
                if t:
                    pe.wait_ge(y_out, (t + 1) // 2)

            need = [max(t for t, tile in enumerate(TILES) if tile[3] < (c + 1) * CW) for c in range(CHUNKS)]
            turns = {(0, 0, 4): [3], (1, 0, 0): [4], (1, 0, 4): [5], (0, 1, 0): [6], (0, 1, 2): [7], (0, 1, 6): [8]}
            assert need == [2, 5, 8] and NT == 9

            def piece(n, c):
                def before(k):
                    if k == 0:
                        turned(need[c])
                    for t in turns.get((n, c, k), ()):
                        turn_input(t)
                return chunk((X, Y)[n], c, n, KD, h_hi, h_lo, before, pads=True)

            pe.wait_ge(const_done, 11)
            for t in range(need[0] + 1):
                turn_input(t)
            pe.wait_ge(wlo_done, 1)
            piece(0, 0)
            pe.wait_ge(wlo_done, 2)
            piece(1, 0)
            piece(0, 1)
            piece(0, 2).then_inc(unit_done, 1)
            turn_params()
            piece(1, 1)
            piece(1, 2).then_inc(unit_done, 1)
            with pe.Fori(1, KA) as j:
                unit(N_A, 2, j, x_out, X_A + j, KD, h_hi, h_lo)
                unit(N_A + 1, 2, j, y_out, Y_A + j, KD, h_hi, h_lo)
            with pe.Fori(0, KB // 2) as b:
                unit(N_B, 6, b, x_out, X_B + 3 * b, KD, h_hi, h_lo)
                unit(N_B + 1, 6, b, y_out, Y_B + 3 * b, KD, h_hi, h_lo)
                unit(N_B + 2, 6, b, x_out, X_B + 1 + 3 * b, KD, h_hi, h_lo)
                unit(N_B + 3, 6, b, y_out, Y_B + 1 + 3 * b, KD, h_hi, h_lo)
                unit(N_B + 4, 6, b, x_out, X_B + 2 + 3 * b, KD, h_hi, h_lo)
                unit(N_B + 5, 6, b, y_out, Y_B + 2 + 3 * b, KD, h_hi, h_lo)

            def row_of(src, part):
                def run():
                    if part == 0:
                        for c in range(2):
                            last = pe.matmul(S[:, c, :], ones[:, :], src[:, c * 512:(c + 1) * 512], start=True, stop=True)
                    else:
                        last = pe.matmul(S[:, 0, 0:SW - 1024], ones[:, :], src[:, 1024:SW], start=True, stop=True)
                    last.then_inc(s_full, 1)
                return run

            def mean_row(part):
                def run():
                    if part == 0:
                        pe.wait_ge(ln_step, 3)
                        pe.wait_ge(pads_done, 1)
                    pe.wait_ge(s_out, S_MEAN + part)
                    row_of(e_b, part)()
                return run

            def sum_columns(src):
                for t in range(NT):
                    last = pe.matmul(S[:, 0, t:t + 1], src[:, t * P:(t + 1) * P], ones[:, 0:1], start=True, stop=True)
                last.then_inc(s_full, 1)

            def ln_columns():
                pe.wait_ge(ln_step, 10)
                pe.wait_ge(s_out, S_VAR)
                sum_columns(e_b)

            def ln_row(part):
                def run():
                    if part == 0:
                        pe.wait_ge(ln_step, 11)
                    pe.wait_ge(s_out, S_LNR + part)
                    row_of(diag, part)()
                return run

            def mix_pair(n0, xb, yb, i, q_need, hooks=((), (), (), ())):
                unit(n0, 4, i, x_out, xb + 2 * i, KD, h_hi, h_lo, hooks[0])
                unit(n0 + 1, 4, i, y_out, yb + 2 * i, KD, h_hi, h_lo, hooks[1])
                pe.wait_ge(qlo_done, q_need)
                unit(n0 + 2, 4, i, x_out, xb + 1 + 2 * i, KB, q_hi, q_lo, hooks[2])
                unit(n0 + 3, 4, i, y_out, yb + 1 + 2 * i, KB, q_hi, q_lo, hooks[3])

            with pe.Fori(0, KD // 2 - 1) as i:
                mix_pair(N_P1, X_P1, Y_P1, i, KB)
            mix_pair(N_P1, X_P1, Y_P1, KD // 2 - 1, KB,
                     ((None, None, mean_row(0)), (mean_row(1),), (None, None, ln_columns), (None, ln_row(0), ln_row(1))))

            def turn_residual(t, use, loads, s):
                rows = TILES[t][2] if isinstance(t, int) else P
                pe.wait_ge(xr_in[s], 16 * loads)
                pe.wait_ge(s_out, use)
                for k in range(KD):
                    last = pe.transpose(S[:, k // 4, (k % 4) * P:(k % 4) * P + rows],
                                        xr[0:rows, s * D + k * P:s * D + (k + 1) * P], ident[0:rows, 0:rows])
                last.then_inc(s_full, 1)

            with pe.Fori(0, KD // 2) as i:
                mix_pair(N_P2, X_P2, Y_P2, i, KB + 2 * KA,
                         ((), (), (None, None, lambda: turn_residual(None, S_XT + 2 * i, i + 1, 0)),
                          (None, None, lambda: turn_residual(None, S_XT + 1 + 2 * i, i + 1, 1))))
            pe.wait_ge(wlo_done, N_WO + 1)
            pe.wait_ge(x_out, X_WO)
            for k in range(KD):
                pe.wait_ge(hlo_done, k + 1)
                for c in range(CHUNKS):
                    last = products(X[:, c, third(c)[0] - c * CW:CW], unit_weights(0, k), (h_hi, h_lo), third(c), k,
                                    k == 0, k == KD - 1)
            last.then_inc(unit_done, 1)
            turn_residual(NT - 1, S_XT + NT - 1, KD // 2 + 1, 0)
            unit(N_WO + 1, 2, 0, y_out, Y_WO, KD, h_hi, h_lo)
            with pe.Fori(1, KD // 2 - 1) as i:
                unit(N_WO, 2, i, x_out, X_WO + i, KD, h_hi, h_lo)
                unit(N_WO + 1, 2, i, y_out, Y_WO + i, KD, h_hi, h_lo)
            i = KD // 2 - 1
            unit(N_WO, 2, i, x_out, X_WO + i, KD, h_hi, h_lo)
            unit(N_WO + 1, 2, i, y_out, Y_WO + i, KD, h_hi, h_lo, part=wo_part)

            pe.wait_ge(state_done, 2)
            pe.wait_ge(b_step, B_STEPS * KB)
            pe.wait_ge(s_out, S_STATE)
            for s in range(2):
                pe.transpose(S[0:HA * KA, 0, s * P:(s + 1) * P], state[:, s * HA * KA:(s + 1) * HA * KA], ident[:, :])
            pe.transpose(S[0:2 * H * KB, 0, 2 * P:3 * P], state[:, ST_B:ST_F], ident[:, :]).then_inc(s_full, 1)

            def ffn_in(c):
                return lambda k: pe.wait_ge(hlo_done, KD + KD * c + k + 1)

            def rms_columns():
                pe.wait_ge(stat_step, 1 + KD)
                pe.wait_ge(s_out, S_MS)
                sum_columns(sq2)

            def rms_row(part):
                def run():
                    if part == 0:
                        pe.wait_ge(stat_step, KD + 2)
                    pe.wait_ge(s_out, S_R2 + part)
                    row_of(diag, part)()
                return run

            unit(N_F, 0, 0, x_out, X_F0, KD, h_hi, h_lo, (None, None, rms_columns), before=ffn_in)
            unit(N_F + 1, 0, 0, y_out, Y_F0, KD, h_hi, h_lo, (rms_row(0), rms_row(1)))
            unit(N_F + 2, 0, 0, x_out, X_F0 + 1, KD, h_hi, h_lo)
            unit(N_F + 3, 0, 0, y_out, Y_F0 + 1, KD, h_hi, h_lo)

            def down_weights(k, m):
                return wd_hi[:, k, m * P:(m + 1) * P], wd_lo[:, k, m * P:(m + 1) * P]

            def down(group, x_use, y_use):
                pe.wait_ge(wdlo_done, group + 1)
                pe.wait_ge(qlo_done, KB + 2 * KA + 2 * group + 2)
                for m in range(KD):
                    b, free, uses = ((Y, y_out, y_use), (X, x_out, x_use))[m % 2]
                    pe.wait_ge(free, uses + m // 2)
                    for c in range(CHUNKS):
                        for k in range(2):
                            last = products(b[:, c, third(c)[0] - c * CW:CW], down_weights(k, m), (q_hi, q_lo),
                                            third(c), k, k == 0, k == 1)
                    last.then_inc(down_done, 1)

            def ffn_units(i, **value_unit):
                xb, yb = X_F1 - 6 + 6 * i, Y_F1 - 6 + 6 * i
                unit(N_F, 4, i, x_out, xb, KD, h_hi, h_lo)
                down(i - 1, xb + 1, yb)
                unit(N_F + 1, 4, i, y_out, yb + 4, KD, h_hi, h_lo)
                unit(N_F + 2, 4, i, x_out, xb + 5, KD, h_hi, h_lo)
                unit(N_F + 3, 4, i, y_out, yb + 5, KD, h_hi, h_lo, **value_unit)

            with pe.Fori(1, G - 1) as i:
                ffn_units(i)
            ffn_units(G - 1, part=value_part, cuts=CUTS)

            pe.wait_ge(f_step, F_STEPS * (KF - 1) + 2)
            pe.wait_ge(s_out, S_FST)
            pe.transpose(S[0:2 * H * KF, 0, 0:P], state[:, ST_F:], ident[:, :]).then_inc(s_full, 1)

            def turn_output(t):
                _, _, rows, c0 = TILES[t]
                b, first_bank = OUT_BANKS[t]
                if t == 0:
                    pe.wait_ge(s_out, S_END)
                used = [u for u in range(t) if OUT_BANKS[u] == OUT_BANKS[t]]
                if used:
                    pe.wait_ge(y_done, used[-1] + 1)
                for k in range(KD):
                    added = (t // T3) * KD + k + 1
                    if b is X:
                        added = max(added, CHUNKS * KD - LAST_BANKS + 1 + k // 4)
                    pe.wait_ge(last_added, added)
                    last = pe.transpose(b[0:rows, first_bank + k // 4, (k % 4) * P:(k % 4 + 1) * P],
                                        stream[:, k, c0:c0 + rows], ident[:, :])
                last.then_inc(xt_done, 1)

            pe.wait_ge(wdlo_done, G)
            pe.wait_ge(qlo_done, Q_F + 2 * G - 1)
            for c in range(CHUNKS):
                pe.wait_ge(qlo_part, c + 1)
                for m in range(KD):
                    if (c, m) in TURN_BEFORE:
                        turn_output(TURN_BEFORE.index((c, m)))
                    j = c * KD + m
                    if j >= LAST_BANKS:
                        pe.wait_ge(last_added, j - LAST_BANKS + 1)
                    elif j < CHUNKS:
                        pe.wait_ge(x_out, X_DL)
                    for k in range(2):
                        last = products((X, Y)[j % LAST_BANKS // CHUNKS][:, j % LAST_BANKS % CHUNKS, 0:CUT_LEN[c]],
                                        down_weights(k, m), (q_hi, q_lo), (CUTS[c], CUTS[c + 1]), k, k == 0, k == 1)
                    last.then_inc(down_done, 1)
            for t in range(NT - T3, NT):
                turn_output(t)

        @block.scalar
        def _(act):
            act.wait_ge(const_done, 3)
            act.activation(state_rows[:, 0, 0:NT], half, ACT.Square).then_inc(warm, 1)

            def split_hi(n0, per=0, i=0, k_tiles=KD, first=False):
                s = n0 % 2
                act.wait_ge(w_in[s], 16 * (n0 // 2 + 1) + 16 * (per // 2) * i)
                if not first:
                    act.wait_ge(unit_done, n0 - 1 + per * i)
                act.activation(w_hi[:, s, 0:k_tiles * P], w_raw[:, s, 0:k_tiles * P], ACT.Copy).then_inc(whi_done, 1)

            def square_rows(t):
                rows = TILES[t][2]
                act.wait_ge(x_in[t % 3], 16 * (t // 3 + 1))
                if t:
                    act.wait_ge(ss_done, t)
                act.activation(t1[0:rows, 0:D], x_slot[t % 3][0:rows, :], ACT.Square,
                               accum_out=ss[0:rows, t:t + 1]).then_inc(ss_done, 1)

            def input_hi(t):
                _, _, rows, c0 = TILES[t]
                act.wait_ge(xt_done, t + 1)
                act.activation(h_hi[:, :, c0:c0 + rows], input_banks(t, rows), ACT.Copy).then_inc(hhi_done, 1)

            square_rows(0)
            square_rows(1)
            input_hi(0)
            square_rows(2)
            split_hi(0, first=True)
            input_hi(1)
            square_rows(3)
            input_hi(2)
            square_rows(4)
            split_hi(1, first=True)
            square_rows(5)
            input_hi(3)
            for t in range(4, NT):
                if t + 2 < NT:
                    square_rows(t + 2)
                input_hi(t)
            act.wait_ge(s_full, 1)
            act.activation(cols[:, :], S[:, 0, 0:NC], ACT.Copy).then_inc(s_out, 1)

            def sigmoid(b, dst, bias, n, out):
                act.wait_ge(unit_done, n + 1)
                act.activation(rows3(dst), bank(b), ACT.Sigmoid, bias=bias).then_inc(out, 1)

            with act.Fori(0, KA) as j:
                split_hi(N_A + 2, 2, j)
                act.wait_ge(y_out, Y_A + j)
                sigmoid(X, t0[:, :], 0.0, N_A + 2 * j, x_out)
                split_hi(N_A + 3, 2, j)
            act.wait_ge(y_out, Y_A + KA)
            for s, c0 in enumerate((HA + NP - HA, UW - HA)):
                act.activation(state[:, s * HA * KA:(s + 1) * HA * KA].rearrange("p (r c) -> p c r", c=KA),
                               u_in[:, :, c0:c0 + HA], ACT.Copy).then_inc(state_done, 1)
            with act.Fori(0, KB // 2) as b:
                for u in range(2):
                    bk, out = ((X, x_out), (Y, y_out))[u]
                    nb = N_B + 3 * u
                    split_hi(nb + 2, 6, b)
                    act.wait_ge(*((x_out, X_B + 3 * b), (y_out, Y_B + 3 * b + 1))[u])
                    act.wait_ge(unit_done, nb + 1 + 6 * b)
                    act.activation(rows3(t0[:, :]), bank(bk), ACT.Copy).then_inc(out, 1)
                    split_hi(nb + 3, 6, b)
                    split_hi(nb + 4, 6, b, k_tiles=KD)
                    use = (X_B + 3 * b + 2, Y_B + 3 * b + 3)[u]
                    act.wait_ge((x_out, y_out)[u], use)
                    act.activation(q_hi[:, bass.ds(2 * b + u, 1), H:W], t1[:, H:W].rearrange("p (a n) -> p a n", a=1),
                                   ACT.Copy).then_inc(qhi_done, 1)

            def mix_gates(n0, gate, i, temps_free):
                for u in range(2):
                    split_hi(n0 + 2 + u, 4, i, k_tiles=KB)
                    temps_free(u)
                    sigmoid((X, Y)[u], (t0, t1)[u][:, :], col("b_gate", gate + u + 2 * i), n0 + u + 4 * i,
                            (x_out, y_out)[u])

            def mix_tail(n0, i):
                split_hi(n0 + 4, 4, i)
                split_hi(n0 + 5, 4, i)

            def b_free(i):
                def run(u):
                    act.wait_ge((x_out, y_out)[u], (X_P1, Y_P1)[u] + 2 * i)
                    if u:
                        act.wait_ge(qlo_done, KB)
                return run

            with act.Fori(0, KD // 2 - 1) as i:
                mix_gates(N_P1, KD, i, b_free(i))
                mix_tail(N_P1, i)
            i = KD // 2 - 1

            def copy_row(dst, n, part, scale=1.0, width=CVW):
                act.wait_ge(s_full, n + 1 + part - SKIP)
                lo, hi = (0, 1024) if part == 0 else (1024, width)
                act.activation(dst[:, lo:hi], S_flat[:, 0:hi - lo], ACT.Copy, scale=scale).then_inc(s_out, 1)

            b_free(i)(0)
            split_hi(N_P1 + 2, 4, i, k_tiles=KB)
            sigmoid(X, t0[:, :], col("b_gate", KD + 2 * i), N_P1 + 4 * i, x_out)
            copy_row(e_c, S_MEAN, 0, 1.0 / DA)
            copy_row(e_c, S_MEAN, 1, 1.0 / DA)
            for c in range(KA):
                act.wait_ge(ln_step, 3 + c + 1)
                if c >= 2:
                    act.wait_ge(ln_step, 3 + KA + c - 1)
                act.activation(sq[c % 2], cv[:, c, :], ACT.Square).then_inc(sq_done, 1)
            split_hi(N_P1 + 3, 4, i, k_tiles=KB)
            b_free(i)(1)
            sigmoid(Y, t1[:, :], col("b_gate", KD + 1 + 2 * i), N_P1 + 1 + 4 * i, y_out)
            split_hi(N_P1 + 4, 4, i)
            copy_row(e_c, S_LNR, 0)
            split_hi(N_P1 + 5, 4, i)
            copy_row(e_c, S_LNR, 1)
            act.wait_ge(unit_done, N_P2)
            for c in range(KA):
                act.wait_ge(ln_step, 11 + c + 1)
                act.activation(cv[:, c, :], cv[:, c, :], ACT.Silu, scale=col("ln_a_g", c),
                               bias=col("ln_a_b", c)).then_inc(silu_done, 1)
            for c in range(KA):
                act.wait_ge(silu_done, c + 1)
                for a, b, n in ((0, P0, NP), (CS, S0, NS)):
                    act.activation(q_hi[:, c, b:b + n], cv[:, c, a:a + n], ACT.Copy).then_inc(qhi_done, 1)

            def a_free(i):
                def run(u):
                    act.wait_ge(wlo_done, N_P2 + 3 + 4 * i)
                    act.wait_ge((x_out, y_out)[u], (X_P2, Y_P2)[u] + 2 * i)
                return run

            def load_x(t, s, turned_before):
                act.wait_ge(s_full, turned_before)
                act.dma_start(xr[:, s * D:(s + 1) * D], x_rows[0][bass.ds(t * P, P), :]).then_inc(xr_in[s], 16)

            def residual(t, c0, rows, use):
                act.wait_ge(s_full, use + 1 - SKIP)
                act.wait_ge(qlo_done, KB + 2 * KA)
                act.activation(stream[:, :, bass.ds(c0, rows)],
                               S[:, :, :].rearrange("p b (k n) -> p (b k) n", n=P)[:, :, 0:rows],
                               ACT.Copy).then_inc(s_out, 1)

            def merged_hi(k):
                act.wait_ge(prod_done, k + 1)
                act.activation(h_hi[:, k, :], merged[:, k, :], ACT.Copy).then_inc(hhi_done, 1)

            def merge_pair(i, last=False):
                load_x(2 * i, 0, S_XT - SKIP + 2 * i)
                load_x(2 * i + 1, 1, S_XT - SKIP + 2 * i)
                mix_gates(N_P2, 0, i, a_free(i))
                if last:
                    for k in range(KD - 2):
                        merged_hi(k)
                for u in range(2):
                    split_hi(N_P2 + 4 + u, 4, i)
                    residual(2 * i + u, P0 + (2 * i + u) * P, P, S_XT + 2 * i + u)
                    if last:
                        merged_hi(KD - 2 + u)

            with act.Fori(0, KD // 2 - 1) as i:
                merge_pair(i)
            merge_pair(KD // 2 - 1, last=True)
            act.wait_ge(s_full, S_XT - SKIP + NT - 1)
            act.dma_start(xr[0:NS, 0:D], x_rows[1][0:NS, :]).then_inc(xr_in[0], 16)
            residual(NT - 1, S0, NS, S_XT + NT - 1)

            def square_stream(i, u):
                act.wait_ge((x_out, y_out)[u], (X_WO, Y_WO)[u] + i + 1)
                act.activation((t0, t1)[u][:, :], res[:, bass.ds((2 * i + u) * W, W)], ACT.Square).then_inc(sq_done, 1)

            with act.Fori(0, KD // 2 - 1) as i:
                for u in range(2):
                    split_hi(N_WO + 2 + u, 2, i)
                    square_stream(i, u)
            split_hi(N_WO + 2, 2, KD // 2 - 1)
            square_stream(KD // 2 - 1, 0)
            for c in range(CHUNKS):
                act.wait_ge(*last_wo(c))
                for k in range(KD):
                    if k == KD - 1:
                        act.wait_ge(*last_wo_added(c))
                    act.activation(h_hi[:, k, c * CW:(c + 1) * CW], stream[:, k, c * CW:(c + 1) * CW], ACT.Copy,
                                   scale=col("norm2_g", k)).then_inc(hhi_done, 1)
            split_hi(N_WO + 3, 2, KD // 2 - 1)
            square_stream(KD // 2 - 1, 1)
            act.wait_ge(s_full, S_STATE + 1 - SKIP)
            act.activation(state_rows[0:HA * KA, 0:2, :].rearrange("p a n -> p (a n)"), S[0:HA * KA, 0, 0:2 * P],
                           ACT.Copy).then_inc(state_done, 1)
            act.activation(state_rows[0:2 * H * KB, 2, :], S[0:2 * H * KB, 0, 2 * P:3 * P], ACT.Copy).then_inc(s_out, 1)

            def silu(f):
                act.wait_ge(f_step, F_STEPS * f + 5)
                act.activation(sl, t1[:, :], ACT.Silu).then_inc(silu_done, 1)

            def ffn_hi(f, u, out, use):
                act.wait_ge(out, use)
                act.activation(q_hi[:, u, :], ac, ACT.Copy).then_inc(qhi_done, 1)

            def split_down(g):
                act.wait_ge(wd_in, 16 * g + 16)
                act.wait_ge(down_done, KD * g)
                act.activation(wd_hi[:, :, :].rearrange("p k c -> p (k c)"), wd_raw, ACT.Copy).then_inc(wdhi_done, 1)

            split_hi(N_F + 2)
            copy_row(rb2, S_R2, 0, 1.0, W)
            copy_row(rb2, S_R2, 1, 1.0, W)
            silu(0)
            split_hi(N_F + 3)
            split_down(0)
            ffn_hi(0, 0, y_out, Y_F0 + 1)
            split_hi(N_F + 4)
            silu(1)
            split_hi(N_F + 5)
            ffn_hi(1, 1, y_out, Y_F0 + 2)
            with act.Fori(1, G - 1) as i:
                yb = Y_F1 - 6 + 6 * i
                split_hi(N_F + 2, 4, i)
                silu(2 * i)
                split_hi(N_F + 3, 4, i)
                split_down(i)
                ffn_hi(2 * i, 0, y_out, yb + 5)
                split_hi(N_F + 4, 4, i)
                silu(2 * i + 1)
                split_hi(N_F + 5, 4, i)
                ffn_hi(2 * i + 1, 1, y_out, yb + 6)
            i = G - 1
            yb = Y_F1 - 6 + 6 * i
            split_hi(N_F + 2, 4, i)
            silu(2 * i)
            split_hi(N_F + 3, 4, i)
            split_down(i)
            ffn_hi(2 * i, 0, y_out, yb + 5)
            silu(2 * i + 1)
            for c in range(CHUNKS):
                act.wait_ge(ac_part, c + 1)
                act.activation(q_hi[:, 1, CUTS[c]:CUTS[c + 1]], ac[:, CUTS[c]:CUTS[c + 1]], ACT.Copy).then_inc(qhi_part, 1)
            act.wait_ge(s_full, S_FST + 1 - SKIP)
            act.activation(state_rows[0:2 * H * KF, 3, :], S[0:2 * H * KF, 0, 0:P], ACT.Copy).then_inc(s_out, 1)
            for t, (_, _, rows, _) in enumerate(TILES):
                act.wait_ge(xt_done, NT + t + 1)
                act.wait_ge(ss_done, NT + t)
                act.activation(t0[0:rows, 0:D], output_banks(t), ACT.Square,
                               accum_out=ss[0:rows, t:t + 1]).then_inc(ss_done, 1)

        @block.vector
        def _(dve):
            def sub(out, full, hi, done):
                dve.tensor_tensor(out, full, hi.bitcast(F32), ALU.subtract).then_inc(done, 1)

            def split_lo(n0, per=0, i=0, k_tiles=KD):
                s, n = n0 % 2, k_tiles * P
                dve.wait_ge(whi_done, n0 + 1 + per * i)
                sub(w_lo[:, s, 0:n], w_raw[:, s, 0:n], w_hi[:, s, 0:n], wlo_done)

            def normalise(t):
                rows = TILES[t][2]
                dve.wait_ge(rs_done, t + 1)
                if t >= XHAT:
                    dve.wait_ge(xt_done, t - XHAT + 1)
                dve.scalar_tensor_tensor(mid[0:rows, (t % XHAT) * D:(t % XHAT + 1) * D], x_slot[t % 3][0:rows, :],
                                         rs[0:rows, t:t + 1], g1_row[0:rows, :], ALU.mult,
                                         ALU.mult).then_inc(xhat_done, 1)

            def input_lo(t):
                _, _, rows, c0 = TILES[t]
                dve.wait_ge(hhi_done, t + 1)
                sub(h_lo[:, :, c0:c0 + rows], input_banks(t, rows), h_hi[:, :, c0:c0 + rows], y_out if t % 2 else s_out)

            dve.wait_ge(g1_in, 16)
            normalise(0)
            normalise(1)
            input_lo(0)
            normalise(2)
            input_lo(1)
            split_lo(0)
            input_lo(2)
            normalise(3)
            normalise(4)
            split_lo(1)
            for t in range(3, NT):
                input_lo(t)
                if t + 2 < NT:
                    normalise(t + 2)
            dve.wait_ge(const_done, 11)
            dve.wait_ge(s_out, S_COLS + 1)
            dve.tensor_copy(u_in[:, :, US - HA:US],
                            cols[:, C["cache_conv_a"]:C["cache_conv_a"] + HA * KA].rearrange("p (r c) -> p c r", c=KA)
                            ).then_inc(hist_done, 1)
            dve.memset(res[:, EB:EB + H], 0.0).then_inc(hist_done, 1)

            def first_tap(c):
                dve.wait_ge(hist_done, 2)
                dve.tensor_scalar(res[:, bass.ds(c * CVW, CVW)], mid[:, bass.ds(U_AT + c * UW, CVW)],
                                  col("dw_a", c), col("b_dw_a", c), ALU.mult, ALU.add).then_inc(tap_done, 1)

            def tap(c, k):
                dve.wait_ge(tap_done, c * TAPS_A + k)
                dst = res[:, bass.ds(c * CVW, CVW)]
                dve.scalar_tensor_tensor(dst, mid[:, bass.ds(U_AT + c * UW + k, CVW)], col("dw_a", k * KA + c), dst,
                                         ALU.mult, ALU.add).then_inc(tap_done, 1)

            def glu(j):
                dve.wait_ge(x_out, X_A + j + 1)
                dve.wait_ge(unit_done, N_A + 2 * j + 2)
                base = U_AT + j * UW + HA - H
                cut = (CHUNKS - 1) * CW
                end = S0 - H - cut
                dve.tensor_tensor(mid[:, bass.ds(base, cut)].rearrange("p (c n) -> p c n", c=CHUNKS - 1),
                                  Y[:, 0:CHUNKS - 1, 0:CW],
                                  t0[:, 0:cut].rearrange("p (c n) -> p c n", c=CHUNKS - 1), ALU.mult).then_inc(u_part, 1)
                dve.tensor_tensor(mid[:, bass.ds(base + cut, end)], Y[:, CHUNKS - 1, 0:end], t0[:, cut:cut + end],
                                  ALU.mult).then_inc(u_part, 1)
                dve.tensor_tensor(mid[:, bass.ds(U_AT + j * UW + US, NS)], Y[:, CHUNKS - 1, CW - NS:CW], t0[:, S0:W],
                                  ALU.mult).then_inc(y_out, 1)

            split_lo(N_A + 2)
            glu(0)
            split_lo(N_A + 3)
            dve.wait_ge(y_out, Y_A + 1)
            first_tap(0)
            per = (TAPS_A - 1) // (KA - 1)
            with dve.Fori(1, KA) as j:
                for r in range(per // 2):
                    tap(0, 1 - per + r + per * j)
                split_lo(N_A + 2, 2, j)
                for r in range(per // 2, per):
                    tap(0, 1 - per + r + per * j)
                glu(j)
                split_lo(N_A + 3, 2, j)

            def mixer_b(b, u, taps):
                nb, c = N_B + 3 * u, 2 * b + u
                val, val_out, gate, gate_out = ((Y, y_out, X, x_out), (X, x_out, Y, y_out))[u]
                c_out, c_use = ((x_out, X_B + 3 * b + 1), (y_out, Y_B + 3 * b + 2))[u]
                v_use = (Y_B + 3 * b + 1, X_B + 3 * b + 3)[u]
                step = B_STEPS * u + 2 * B_STEPS * b
                split_lo(nb + 2, 6, b)
                taps(3 * u)
                dve.wait_ge(c_out, c_use)
                dve.wait_ge(unit_done, nb + 2 + 6 * b)
                dve.tensor_tensor(rows3(bw_in), bank(val), rows3(t0[:, :]), ALU.mult).then_inc(val_out, 1)
                split_lo(nb + 3, 6, b)
                dve.wait_ge(val_out, v_use)
                dve.tensor_copy(bw_in[:, S0 - H:S0].rearrange("p (r a) -> p r a", a=1),
                                every(cols, C["cache_conv_b"], H, KB, c)).then_inc(b_step, 1)
                for s, c0 in enumerate((P0 + NP - H, W - H)):
                    st = dve.tensor_copy(every(state, ST_B + s * H * KB, H, KB, c),
                                         bw_in[:, c0:c0 + H].rearrange("p (r a) -> p r a", a=1))
                st.then_inc(b_step, 1)
                dve.wait_ge(b_step, step + 1)
                out = v_row[:, H:W]
                dve.tensor_scalar(out, bw_in[:, 0:W - H], col("dw_b", c), None, ALU.mult).then_inc(b_step, 1)
                for k in range(1, TAPS_B):
                    dve.wait_ge(b_step, step + 2 + k)
                    dve.scalar_tensor_tensor(out, bw_in[:, k:k + W - H], col("dw_b", k * KB + c), out,
                                             ALU.mult, ALU.add).then_inc(b_step, 1)
                taps(3 * u + 1)
                split_lo(nb + 4, 6, b)
                dve.wait_ge(b_step, step + B_STEPS)
                dve.wait_ge(unit_done, nb + 3 + 6 * b)
                dve.tensor_tensor(rows3(t1[:, :]), bank(gate), rows3(v_row), ALU.mult).then_inc(gate_out, 1)
                taps(3 * u + 2)
                dve.wait_ge(qhi_done, c + 1)
                sub(q_lo[:, bass.ds(c, 1), H:W], t1[:, H:W].rearrange("p (a n) -> p a n", a=1),
                    q_hi[:, bass.ds(c, 1), H:W], qlo_done)

            dve.wait_ge(y_out, Y_A + KA)
            per6 = (TAPS_A - 1) // 6
            with dve.Fori(0, KB // 2) as b:
                first_tap(b + 1)

                def taps(place):
                    for k in range(1 + per6 * place, 1 + per6 * (place + 1)):
                        tap(b + 1, k)

                for u in range(2):
                    mixer_b(b, u, taps)

            def merge_b(u, i, n):
                bk, out = ((X, x_out), (Y, y_out))[u]
                dve.wait_ge(unit_done, n + 1)
                dve.wait_ge(out, (X_P1, Y_P1)[u] + 1 + 2 * i)
                dve.tensor_tensor(mid[:, bass.ds((2 * i + u) * W, W)].rearrange("p (c n) -> p c n", c=CHUNKS),
                                  bank(bk), rows3((t0, t1)[u][:, :]), ALU.mult).then_inc(out, 1)

            first_tap(KA - 1)
            with dve.Fori(0, KD // 2 - 1) as i:
                k = 0
                for u, taps_here in ((0, 3), (1, 3), (2, 2), (3, 2)):
                    split_lo(N_P1 + 2 + u, 4, i, k_tiles=KB if u < 2 else KD)
                    if u >= 2:
                        merge_b(u - 2, i, N_P1 + u + 4 * i)
                    for _ in range(taps_here):
                        tap(KA - 1, 1 + k + per * i)
                        k += 1
            i = KD // 2 - 1
            dve.wait_ge(tap_done, KA * TAPS_A)
            dve.tensor_tensor(e_b[:, 0:CVW], cv[:, 0, :], cv[:, 1, :], ALU.add).then_inc(ln_step, 1)
            for c in range(2, KA):
                dve.wait_ge(ln_step, c - 1)
                dve.tensor_tensor(e_b[:, 0:CVW], e_b[:, 0:CVW], cv[:, c, :], ALU.add).then_inc(ln_step, 1)
            split_lo(N_P1 + 2, 4, i, k_tiles=KB)
            dve.wait_ge(s_out, S_MEAN + 2)
            for c in range(KA):
                dve.tensor_tensor(cv[:, c, :], cv[:, c, :], e_c[:, 0:CVW], ALU.subtract).then_inc(ln_step, 1)
            dve.wait_ge(sq_done, 2)
            dve.tensor_tensor(e_b[:, 0:CVW], sq[0], sq[1], ALU.add).then_inc(ln_step, 1)
            for c in range(2, KA):
                dve.wait_ge(sq_done, c + 1)
                dve.wait_ge(ln_step, 3 + KA + c - 1)
                dve.tensor_tensor(e_b[:, 0:CVW], e_b[:, 0:CVW], sq[c % 2], ALU.add).then_inc(ln_step, 1)
            split_lo(N_P1 + 3, 4, i, k_tiles=KB)

            def moments(use, n, eps):
                dve.wait_ge(s_full, use + 1 - SKIP)
                dve.tensor_scalar(m9, S[:, 0, 0:NT], 1.0 / n, eps, ALU.mult, ALU.add).then_inc(s_out, 1)

            def diagonals(done, count):
                dve.wait_ge(rs_done, count)
                dve.tensor_tensor(diag.rearrange("p (t n) -> p t n", t=NT),
                                  ident[:, :].rearrange("p (a n) -> p a n", a=1).to_broadcast([P, NT, P]),
                                  r9.rearrange("p (t a) -> p t a", a=1).to_broadcast([P, NT, P]),
                                  ALU.mult).then_inc(done, 1)

            moments(S_VAR, DA, LN_EPS)
            split_lo(N_P1 + 4, 4, i)
            merge_b(0, i, N_P1 + 2 + 4 * i)
            diagonals(ln_step, NT + 1)
            split_lo(N_P1 + 5, 4, i)
            merge_b(1, i, N_P1 + 3 + 4 * i)
            dve.wait_ge(s_out, S_LNR + 2)
            for c in range(KA):
                dve.tensor_tensor(cv[:, c, :], cv[:, c, :], e_c[:, 0:CVW], ALU.mult).then_inc(ln_step, 1)
            for c in range(KA):
                for u, (a, b, n) in enumerate(((0, P0, NP), (CS, S0, NS))):
                    dve.wait_ge(qhi_done, KB + 2 * c + u + 1)
                    sub(q_lo[:, c, b:b + n], cv[:, c, a:a + n], q_hi[:, c, b:b + n], qlo_done)

            def merge_a(u, i):
                bk, out = ((X, x_out), (Y, y_out))[u]
                t = (t0, t1)[u]
                dve.wait_ge(out, (X_P2, Y_P2)[u] + 1 + 2 * i)
                dve.wait_ge(unit_done, N_P2 + 3 + u + 4 * i)
                dve.tensor_tensor(rows3(t[:, :]), bank(bk), rows3(t[:, :]), ALU.mult).then_inc(out, 1)
                dve.wait_ge(out, (X_P2, Y_P2)[u] + 2 + 2 * i)
                m = mid[:, bass.ds((2 * i + u) * W, W)]
                dve.tensor_tensor(m, m, t[:, :], ALU.add).then_inc(prod_done, 1)

            def merged_lo(k):
                dve.wait_ge(hhi_done, NT + k + 1)
                sub(h_lo[:, k, :], merged[:, k, :], h_hi[:, k, :], hlo_done)

            with dve.Fori(0, KD // 2 - 1) as i:
                for u in range(4):
                    split_lo(N_P2 + 2 + u, 4, i, k_tiles=KB if u < 2 else KD)
                    if u >= 2:
                        merge_a(u - 2, i)
            i = KD // 2 - 1
            split_lo(N_P2 + 2, 4, i, k_tiles=KB)
            split_lo(N_P2 + 3, 4, i, k_tiles=KB)
            for k in range(KD - 2):
                merged_lo(k)
            split_lo(N_P2 + 4, 4, i)
            merge_a(0, i)
            merged_lo(KD - 2)
            merge_a(1, i)
            split_lo(N_P2 + 5, 4, i)
            merged_lo(KD - 1)

            dve.wait_ge(s_out, S_XT + NT)
            dve.wait_ge(pads_done, 3)

            def add_residual(i, u):
                bk, out = ((X, x_out), (Y, y_out))[u]
                dve.wait_ge(unit_done, N_WO + 1 + u + 2 * i)
                x = res[:, bass.ds((2 * i + u) * W, W)]
                dve.tensor_tensor(x.rearrange("p (c n) -> p c n", c=CHUNKS), bank(bk),
                                  x.rearrange("p (c n) -> p c n", c=CHUNKS), ALU.add).then_inc(out, 1)

            def add_squares(i, u):
                dve.wait_ge(sq_done, KA + 1 + u + 2 * i)
                dve.wait_ge(stat_step, 1 + u + 2 * i)
                dve.tensor_tensor(sq2[:, 0:W], sq2[:, 0:W], (t0, t1)[u][:, :], ALU.add).then_inc(stat_step, 1)

            with dve.Fori(0, KD // 2 - 1) as i:
                for u in range(2):
                    split_lo(N_WO + 2 + u, 2, i)
                    add_residual(i, u)
                    add_squares(i, u)
            i = KD // 2 - 1
            split_lo(N_WO + 2, 2, i)
            add_residual(i, 0)
            add_squares(i, 0)
            for c in range(CHUNKS):
                part = slice(c * CW, (c + 1) * CW)
                dve.wait_ge(*last_wo(c))
                dve.tensor_tensor(stream[:, KD - 1, part], Y[:, c, 0:CW], stream[:, KD - 1, part],
                                  ALU.add).then_inc(last_wo_added(c)[0], 1)
                for k in range(KD):
                    dve.wait_ge(hhi_done, NT + KD + c * KD + k + 1)
                    dve.scalar_tensor_tensor(h_lo[:, k, part], stream[:, k, part], col("norm2_g", k),
                                             h_hi[:, k, part].bitcast(F32), ALU.mult, ALU.subtract).then_inc(hlo_done, 1)
            split_lo(N_WO + 3, 2, i)
            add_squares(i, 1)
            moments(S_MS, D, RMS_EPS)
            diagonals(stat_step, NT + 2)

            def gate(f, n, use):
                dve.wait_ge(unit_done, n + 1)
                dve.tensor_tensor(rows3(t0[:, :]), bank(X), rows3(rb2), ALU.mult).then_inc(x_out, 1)
                dve.wait_ge(x_out, use + 1)
                dve.tensor_copy(t0[:, S0 - H:S0].rearrange("p (r a) -> p r a", a=1),
                                every(cols, C["cache_ffn_conv"], H, KF, f)).then_inc(f_step, 1)
                for s, c0 in enumerate((P0 + NP - H, W - H)):
                    st = dve.tensor_copy(every(state, ST_F + s * H * KF, H, KF, f),
                                         t0[:, c0:c0 + H].rearrange("p (r a) -> p r a", a=1))
                st.then_inc(f_step, 1)

            def conv(f, k):
                out = t1[:, H:W]
                dve.wait_ge(f_step, F_STEPS * f + (1 if k == 0 else 2 + k))
                if k == 0:
                    dve.tensor_scalar(out, t0[:, 0:W - H], col("dw_f", f), None, ALU.mult).then_inc(f_step, 1)
                else:
                    dve.scalar_tensor_tensor(out, t0[:, k:k + W - H], col("dw_f", k * KF + f), out,
                                             ALU.mult, ALU.add).then_inc(f_step, 1)

            def scale_silu(f):
                dve.wait_ge(silu_done, KA + 1 + f)
                dve.tensor_tensor(sl, sl, rb2, ALU.mult).then_inc(f_step, 1)

            def value(f, n):
                dve.wait_ge(f_step, F_STEPS * f + F_STEPS)
                dve.wait_ge(unit_done, n + 1)
                dve.tensor_tensor(rows3(ac), bank(Y), rows3(sl), ALU.mult).then_inc(y_out, 1)

            def ffn_lo(f, u):
                dve.wait_ge(qhi_done, Q_F + f + 1)
                sub(q_lo[:, u, :], ac, q_hi[:, u, :], qlo_done)

            def split_down(g):
                dve.wait_ge(wdhi_done, g + 1)
                sub(wd_lo[:, :, :].rearrange("p k c -> p (k c)"), wd_raw,
                    wd_hi[:, :, :].rearrange("p k c -> p (k c)"), wdlo_done)

            def add_down(g, m):
                bk, out = ((Y, y_out), (X, x_out))[m % 2]
                dve.wait_ge(down_done, KD * g + m + 1)
                x = rows3(stream[:, m, :])
                dve.tensor_tensor(x, bank(bk), x, ALU.add).then_inc(out, 1)

            split_lo(N_F + 2)
            dve.wait_ge(s_out, S_R2 + 2)
            gate(0, N_F, X_F0)
            for k in range(TAPS_F):
                conv(0, k)
            split_lo(N_F + 3)
            scale_silu(0)
            value(0, N_F + 1)
            split_down(0)
            ffn_lo(0, 0)
            split_lo(N_F + 4)
            gate(1, N_F + 2, X_F0 + 1)
            for k in range(TAPS_F):
                conv(1, k)
            split_lo(N_F + 5)
            scale_silu(1)
            value(1, N_F + 3)
            ffn_lo(1, 1)

            def ffn_group(i, last=False):
                xb = X_F1 - 6 + 6 * i
                gate(2 * i, N_F + 4 * i, xb)
                split_lo(N_F + 2, 4, i)
                conv(2 * i, 0)
                for m in range(KD):
                    add_down(i - 1, m)
                    if m + 1 < TAPS_F:
                        conv(2 * i, m + 1)
                    if m == 4:
                        scale_silu(2 * i)
                split_lo(N_F + 3, 4, i)
                split_down(i)
                value(2 * i, N_F + 1 + 4 * i)
                ffn_lo(2 * i, 0)
                if not last:
                    split_lo(N_F + 4, 4, i)
                gate(2 * i + 1, N_F + 2 + 4 * i, xb + 5)
                for k in range(TAPS_F):
                    conv(2 * i + 1, k)
                if not last:
                    split_lo(N_F + 5, 4, i)
                scale_silu(2 * i + 1)
                if not last:
                    value(2 * i + 1, N_F + 3 + 4 * i)
                    ffn_lo(2 * i + 1, 1)

            with dve.Fori(1, G - 1) as i:
                ffn_group(i)
            ffn_group(G - 1, last=True)
            dve.wait_ge(f_step, F_STEPS * KF)
            for c in range(CHUNKS):
                part = slice(CUTS[c], CUTS[c + 1])
                dve.wait_ge(*((value_part, c + 1) if c < CHUNKS - 1 else (unit_done, N_F + 4 * G)))
                dve.tensor_tensor(ac[:, part], Y[:, c, 0:CUT_LEN[c]], sl[:, part], ALU.mult).then_inc(ac_part, 1)
                dve.wait_ge(qhi_part, c + 1)
                sub(q_lo[:, 1, part], ac[:, part], q_hi[:, 1, part], qlo_part)

            def final_norm(t):
                rows = TILES[t][2]
                dve.wait_ge(rs_done, NT + 2 + t + 1)
                dve.scalar_tensor_tensor(out_rows[0:rows, t, :], output_banks(t), rs[0:rows, t:t + 1],
                                         gf_row[0:rows, :], ALU.mult, ALU.mult).then_inc(y_done, 1)

            dve.wait_ge(gf_in, 16)
            for c in range(CHUNKS):
                part = slice(CUTS[c], CUTS[c + 1])
                for m in range(KD):
                    j = c * KD + m
                    dve.wait_ge(down_done, KD * (G - 1) + j + 1)
                    dve.tensor_tensor(stream[:, m, part],
                                      (X, Y)[j % LAST_BANKS // CHUNKS][:, j % LAST_BANKS % CHUNKS, 0:CUT_LEN[c]],
                                      stream[:, m, part], ALU.add).then_inc(last_added, 1)
                    if (c, m) in NORM_AFTER:
                        final_norm(NORM_AFTER.index((c, m)))
            for t in range(len(NORM_AFTER), NT):
                final_norm(t)


_INS = ["x_prompt", "x_sample", "cache_conv_a", "cache_conv_b", "cache_ffn_conv", "norm1_g", "w_in", "b_gate",
        "dw_a", "b_dw_a", "ln_a_g", "ln_a_b", "w_a_out", "dw_b", "w_b_out", "w_o", "norm2_g", "w_up", "dw_f",
        "w_down", "final_g"]
_OUTS = ["y_prompt", "y_sample", "new_conv_a_p", "new_conv_b_p", "new_ffn_conv_p",
         "new_conv_a_s", "new_conv_b_s", "new_ffn_conv_s"]


def kernel(**inputs):
    import concourse.bacc as bacc
    import numpy as np
    from concourse.bass_utils import run_bass_kernel_spmd

    nc = bacc.Bacc("TRN2", target_bir_lowering=False, num_devices=1, dynamic_dma_scratch_size=1024)
    arrays = {f"in_{n}": np.ascontiguousarray(inputs[n]) for n in _INS}
    shapes = {
        "y_prompt": inputs["x_prompt"].shape,
        "y_sample": inputs["x_sample"].shape,
    }
    for name in ("conv_a", "conv_b", "ffn_conv"):
        depth, batch, rows, width = inputs[f"cache_{name}"].shape
        shapes[f"new_{name}_p"] = (depth, inputs["x_prompt"].shape[0], rows, width)
        shapes[f"new_{name}_s"] = (depth, batch, rows, width)
    ins = {n: nc.dram_tensor(f"in_{n}", arrays[f"in_{n}"].shape, F32, kind="ExternalInput").ap() for n in _INS}
    outs = {n: nc.dram_tensor(f"out_{n}", shapes[n], F32, kind="ExternalOutput").ap() for n in _OUTS}
    streaming_encoder(nc, ins, outs)
    got = run_bass_kernel_spmd(nc, [arrays], core_ids=[0])
    return tuple(got.results[0][f"out_{n}"] for n in _OUTS)
```
